# Optimizing a Trainium2 kernel written in Bass

```python
import jax, jax.numpy as jnp
from jax import lax
import numpy as np

D_MODEL = 1024
BATCH = 1
SEQ = 256
DEPTH = 2
DEC_BATCH = 8
DEC_SEQ = 4
PAST_LEN = 1024
PAGE_SIZE = 128

SWA_HEADS = 8
SWA_KV_HEADS = 2
SWA_HEAD_DIM = 64
SWA_GROUP = SWA_HEADS // SWA_KV_HEADS
WINDOW = 128
ROPE_THETA = 10000.0
HG_HEADS = 4
HG_DK = 128
HG_DV = 128
HG_CHUNK = 64
LB_FLOOR = 1e-30
POOL_WINDOWS = (2, 4, 8, 16)
POOL_GROUPS = 4
POOL_GROUP_DIM = 128
POOL_WIDTH = POOL_GROUPS * POOL_GROUP_DIM
POOL_BUF = 15
BRANCH_WIDTH = 512
N_BRANCH = 3
D_FF = 4 * D_MODEL
EPS = 1e-6
NEG = -1e30

SWA_Q = SWA_HEADS * SWA_HEAD_DIM
SWA_KV = SWA_KV_HEADS * SWA_HEAD_DIM
HG_K = HG_HEADS * HG_DK
HG_V = HG_HEADS * HG_DV
GATE_W = N_BRANCH * D_MODEL
P1 = SWA_Q
P2 = P1 + SWA_KV
P3 = P2 + SWA_KV
P4 = P3 + HG_K
P5 = P4 + HG_K
P6 = P5 + HG_V
P7 = P6 + HG_V
P8 = P7 + POOL_WIDTH
D_IN = P8 + GATE_W
SPLIT_POINTS = (P1, P2, P3, P4, P5, P6, P7, P8)

kernel_name = "hybrid_hgrn2_swa_pool_gated_decode_step"

F32 = jnp.float32

def rmsnorm(x, w):
    xf = x.astype(F32)
    y = xf * lax.rsqrt(jnp.mean(xf * xf, axis=-1, keepdims=True) + EPS) * w.astype(F32)
    return y.astype(x.dtype)

def rope(x, pos):
    hd = x.shape[-1]
    inv = jnp.power(ROPE_THETA, -jnp.arange(0, hd, 2, dtype=F32) / hd)
    ang = pos[:, None] * inv[None, :]
    cos = jnp.cos(ang)[:, None, :]
    sin = jnp.sin(ang)[:, None, :]
    xf = x.astype(F32)
    x1, x2 = xf[..., : hd // 2], xf[..., hd // 2:]
    return jnp.concatenate([x1 * cos - x2 * sin, x2 * cos + x1 * sin], axis=-1).astype(x.dtype)

def sink_softmax(s, mask, sink):
    sink = sink.astype(F32)
    sm = jnp.where(mask, s, NEG)
    m = jnp.maximum(jnp.max(sm, axis=-1, keepdims=True), sink)
    e = jnp.where(mask, jnp.exp(sm - m), 0.0)
    return e / (jnp.sum(e, axis=-1, keepdims=True) + jnp.exp(sink - m))

def swa_prompt(q, k, v, sinks):
    B, T = q.shape[:2]
    nb = T // WINDOW
    qb = q.astype(F32).reshape(B, nb, WINDOW, SWA_KV_HEADS, SWA_GROUP, SWA_HEAD_DIM)

    def with_prev(a):
        a = a.astype(F32).reshape(B, nb, WINDOW, SWA_KV_HEADS, SWA_HEAD_DIM)
        prev = jnp.pad(a, ((0, 0), (1, 0), (0, 0), (0, 0), (0, 0)))[:, :-1]
        return jnp.concatenate([prev, a], axis=2)

    kk = with_prev(k)
    vv = with_prev(v)
    s = jnp.einsum('bnqkgd,bnskd->bnkgqs', qb, kk) * (SWA_HEAD_DIM ** -0.5)
    i = jnp.arange(WINDOW)[:, None]
    j = jnp.arange(2 * WINDOW)[None, :]
    band = (j > i) & (j <= i + WINDOW)
    blk = jnp.arange(nb)[:, None, None]
    mask = band[None] & ((blk > 0) | (j[None] >= WINDOW))
    p = sink_softmax(s, mask[None, :, None, None], sinks.reshape(SWA_KV_HEADS, SWA_GROUP)[:, :, None, None])
    o = jnp.einsum('bnkgqs,bnskd->bnqkgd', p, vv)
    return o.reshape(B, T, SWA_Q).astype(q.dtype)

def swa_sample(q, k, v, k_buf, v_buf, sinks):
    B, T = q.shape[:2]
    WB = k_buf.shape[1]
    kk = jnp.concatenate([k_buf.astype(k.dtype), k], axis=1)
    vv = jnp.concatenate([v_buf.astype(v.dtype), v], axis=1)
    qpos = PAST_LEN + jnp.arange(T)[:, None]
    kpos = PAST_LEN - WB + jnp.arange(WB + T)[None, :]
    mask = (kpos <= qpos) & (qpos - kpos < WINDOW)
    qg = q.astype(F32).reshape(B, T, SWA_KV_HEADS, SWA_GROUP, SWA_HEAD_DIM)
    s = jnp.einsum('btkgd,bskd->bkgts', qg, kk.astype(F32)) * (SWA_HEAD_DIM ** -0.5)
    p = sink_softmax(s, mask, sinks.reshape(SWA_KV_HEADS, SWA_GROUP)[:, :, None, None])
    o = jnp.einsum('bkgts,bskd->btkgd', p, vv.astype(F32))
    return o.reshape(B, T, SWA_Q).astype(q.dtype), kk[:, -WB:], vv[:, -WB:]

def hgrn2(q, logf, kg, inp, S0):
    B, T = q.shape[:2]
    C = min(HG_CHUNK, T)
    pad = (-T) % C
    padw = ((0, 0), (0, pad), (0, 0), (0, 0))
    n = (T + pad) // C

    def chunks(a):
        a = jnp.pad(a, padw)
        return a.reshape(B, n, C, a.shape[2], a.shape[3]).swapaxes(0, 1)

    causal = jnp.tril(jnp.ones((C, C), dtype=bool))[None, :, :, None, None]

    def step(S, xs):
        qc, gc, kc, ic = xs
        G = jnp.cumsum(gc, axis=1)
        o_inter = jnp.einsum('bchd,bhde->bche', qc * jnp.exp(G), S)
        diff = G[:, :, None] - G[:, None, :]
        dec = jnp.where(causal, jnp.exp(jnp.where(causal, diff, 0.0)), 0.0)
        A = jnp.einsum('bthd,btshd,bshd->bhts', qc, dec, kc)
        o_intra = jnp.einsum('bhts,bshe->bthe', A, ic)
        G_last = G[:, -1]
        S_new = jnp.exp(G_last)[..., None] * S + jnp.einsum(
            'bshd,bshe->bhde', kc * jnp.exp(G_last[:, None] - G), ic)
        return S_new, o_inter + o_intra

    S, o = lax.scan(step, S0, (chunks(q), chunks(logf), chunks(kg), chunks(inp)))
    o = o.swapaxes(0, 1).reshape(B, n * C, HG_HEADS, HG_DV)[:, :T]
    return o, S

def pool_mix(u_ext, T, w_pool, scale):
    B, L, _ = u_ext.shape
    uf = u_ext.astype(F32)
    cs = jnp.concatenate([jnp.zeros((B, 1, POOL_WIDTH), F32), jnp.cumsum(uf, axis=1)], axis=1)
    e = jnp.arange(L - T, L)
    outs = []
    for g, w in enumerate(POOL_WINDOWS):
        sl = slice(g * POOL_GROUP_DIM, (g + 1) * POOL_GROUP_DIM)
        hi = cs[:, e + 1, sl]
        lo = cs[:, jnp.maximum(e + 1 - w, 0), sl]
        cnt = jnp.minimum(w, e + 1).astype(F32)[None, :, None]
        outs.append((hi - lo) / cnt - uf[:, e, sl])
    d = jnp.concatenate(outs, axis=-1).reshape(B, T, POOL_GROUPS, POOL_GROUP_DIM)
    y = jnp.einsum('btgc,gcd->btgd', d, w_pool.astype(F32)).reshape(B, T, POOL_WIDTH)
    return (y * scale.astype(F32)).astype(u_ext.dtype)

def decoder_layer(x, pos, lw, st):
    (norm_mix, w_in, q_norm, k_norm, sinks, lb, onorm, pool_w, pool_scale,
     w_branch, w_o, norm_ffn, w_up, w_down) = lw
    B, T, _ = x.shape
    xn = rmsnorm(x, norm_mix)
    z = xn @ w_in
    zq, zk, zv, hq, hf, hi, hg, u, zg = jnp.split(z, SPLIT_POINTS, axis=-1)

    q = rope(rmsnorm(zq.reshape(B, T, SWA_HEADS, SWA_HEAD_DIM), q_norm), pos)
    k = rope(rmsnorm(zk.reshape(B, T, SWA_KV_HEADS, SWA_HEAD_DIM), k_norm), pos)
    v = zv.reshape(B, T, SWA_KV_HEADS, SWA_HEAD_DIM)
    if st is None:
        WB = min(WINDOW, T)
        o_b = swa_prompt(q, k, v, sinks)
        k_new, v_new = k[:, -WB:], v[:, -WB:]
        S0 = jnp.zeros((B, HG_HEADS, HG_DK, HG_DV), F32)
        s_dtype = x.dtype
        u_ext = u
    else:
        S_in, k_buf, v_buf, p_buf = st
        o_b, k_new, v_new = swa_sample(q, k, v, k_buf, v_buf, sinks)
        S0 = S_in.astype(F32)
        s_dtype = S_in.dtype
        u_ext = jnp.concatenate([p_buf.astype(u.dtype), u], axis=1)

    zf = hf.astype(F32).reshape(B, T, HG_HEADS, HG_DK)
    lbh = lb.reshape(HG_HEADS, HG_DK)
    logf = jnp.logaddexp(jnp.log(jnp.maximum(lbh, LB_FLOOR)), jnp.log1p(-lbh) + jax.nn.log_sigmoid(zf))
    kg = (1.0 - lbh) * jax.nn.sigmoid(-zf)
    qh = jax.nn.silu(hq.astype(F32)).reshape(B, T, HG_HEADS, HG_DK)
    ih = hi.astype(F32).reshape(B, T, HG_HEADS, HG_DV)
    o, S_new = hgrn2(qh, logf, kg, ih, S0)
    o = rmsnorm(o, onorm) * jax.nn.silu(hg.astype(F32).reshape(B, T, HG_HEADS, HG_DV))
    o_a = o.reshape(B, T, HG_V).astype(x.dtype)

    o_c = pool_mix(u_ext, T, pool_w, pool_scale)
    p_new = u_ext[:, -POOL_BUF:]

    br = jnp.stack([o_a, o_b, o_c], axis=-2)
    proj = jnp.einsum('btnc,ncd->btnd', br, w_branch)
    gates = jax.nn.sigmoid(zg.reshape(B, T, N_BRANCH, D_MODEL))
    x = x + jnp.sum(gates * proj, axis=-2) @ w_o

    h = rmsnorm(x, norm_ffn) @ w_up
    x = x + jnp.square(jax.nn.relu(h)) @ w_down
    return x, (S_new.astype(s_dtype), k_new, v_new, p_new)

def setup_inputs(seed: int = 0) -> dict:
    key = jax.random.key(seed)
    ks = jax.random.split(key, 20)
    WB = min(WINDOW, PAST_LEN)

    def nrm(k, shape, s):
        return jax.random.normal(k, shape, F32) * s

    return {
        "x_prompt": nrm(ks[0], (BATCH, SEQ, D_MODEL), 1.0),
        "x_sample": nrm(ks[1], (DEC_BATCH, DEC_SEQ, D_MODEL), 1.0),
        "state_hgrn": nrm(ks[2], (DEPTH, DEC_BATCH, HG_HEADS, HG_DK, HG_DV), 0.5),
        "cache_swa_k": nrm(ks[3], (DEPTH, DEC_BATCH, WB, SWA_KV_HEADS, SWA_HEAD_DIM), 1.0),
        "cache_swa_v": nrm(ks[4], (DEPTH, DEC_BATCH, WB, SWA_KV_HEADS, SWA_HEAD_DIM), 1.0),
        "state_pool": nrm(ks[5], (DEPTH, DEC_BATCH, POOL_BUF, POOL_WIDTH), 1.0),
        "norm_mix": 1.0 + nrm(ks[6], (DEPTH, D_MODEL), 0.05),
        "w_in": nrm(ks[7], (DEPTH, D_MODEL, D_IN), D_MODEL ** -0.5),
        "q_norm": 1.0 + nrm(ks[8], (DEPTH, SWA_HEAD_DIM), 0.05),
        "k_norm": 1.0 + nrm(ks[9], (DEPTH, SWA_HEAD_DIM), 0.05),
        "attn_sinks": nrm(ks[10], (DEPTH, SWA_HEADS), 0.5),
        "hgrn_lb": nrm(ks[11], (DEPTH, HG_K), 0.1),
        "hgrn_onorm": 1.0 + nrm(ks[12], (DEPTH, HG_DV), 0.05),
        "pool_w": nrm(ks[13], (DEPTH, POOL_GROUPS, POOL_GROUP_DIM, POOL_GROUP_DIM), POOL_GROUP_DIM ** -0.5),
        "pool_scale": 1.0 + nrm(ks[14], (DEPTH, POOL_WIDTH), 0.1),
        "w_branch": nrm(ks[15], (DEPTH, N_BRANCH, BRANCH_WIDTH, D_MODEL), BRANCH_WIDTH ** -0.5),
        "w_o": nrm(ks[16], (DEPTH, D_MODEL, D_MODEL), D_MODEL ** -0.5),
        "norm_ffn": 1.0 + nrm(ks[17], (DEPTH, D_MODEL), 0.05),
        "w_up": nrm(ks[18], (DEPTH, D_MODEL, D_FF), D_MODEL ** -0.5),
        "w_down": nrm(ks[19], (DEPTH, D_FF, D_MODEL), D_FF ** -0.5),
    }

def reference(x_prompt, x_sample, state_hgrn, cache_swa_k, cache_swa_v, state_pool,
              norm_mix, w_in, q_norm, k_norm, attn_sinks, hgrn_lb, hgrn_onorm,
              pool_w, pool_scale, w_branch, w_o, norm_ffn, w_up, w_down):
    lbp = jax.nn.softmax(hgrn_lb.astype(F32), axis=0)
    lower = jnp.maximum(jnp.cumsum(lbp, axis=0) - lbp[0], 0.0)
    pos_p = jnp.arange(x_prompt.shape[1], dtype=F32)
    pos_s = jnp.arange(x_sample.shape[1], dtype=F32) + PAST_LEN
    hp, hs = x_prompt, x_sample
    sp = ([], [], [], [])
    ss = ([], [], [], [])
    for l in range(DEPTH):
        lw = (norm_mix[l], w_in[l], q_norm[l], k_norm[l], attn_sinks[l], lower[l], hgrn_onorm[l],
              pool_w[l], pool_scale[l], w_branch[l], w_o[l], norm_ffn[l], w_up[l], w_down[l])
        hp, new_p = decoder_layer(hp, pos_p, lw, None)
        hs, new_s = decoder_layer(hs, pos_s, lw, (state_hgrn[l], cache_swa_k[l], cache_swa_v[l], state_pool[l]))
        for lst, a in zip(sp, new_p):
            lst.append(a)
        for lst, a in zip(ss, new_s):
            lst.append(a)
    return (hp, hs,
            jnp.stack(sp[0]), jnp.stack(sp[1]), jnp.stack(sp[2]), jnp.stack(sp[3]),
            jnp.stack(ss[0]), jnp.stack(ss[1]), jnp.stack(ss[2]), jnp.stack(ss[3]))


_drawn_inputs = setup_inputs


def setup_inputs(seed=0):
    import zlib

    import numpy as np

    out = dict(_drawn_inputs(seed))
    spreads = {}
    factors = {'q_norm': 8.0, 'attn_sinks': 8.0, 'hgrn_onorm': 3.144}
    for name, (base, spread) in spreads.items():
        noise = np.random.default_rng([zlib.crc32(name.encode()), seed]).standard_normal(out[name].shape)
        drawn = base * np.exp(spread * noise) if base else spread * noise
        out[name] = __import__('jax').numpy.asarray(drawn.astype(out[name].dtype))
    for name, factor in factors.items():
        out[name] = (out[name] * factor).astype(out[name].dtype)
    return out
```

```python
from contextlib import ExitStack

import numpy as np

import concourse.bass as bass
from concourse import mybir

F32 = mybir.dt.float32
F32R = mybir.dt.float32r
U8 = mybir.dt.uint8
ACT = mybir.ActivationFunctionType
ALU = mybir.AluOpType
AX_X = mybir.AxisListType.X

P = 128
DEPTH = 2
D_MODEL = 1024
KT = D_MODEL // P
NP = 256
B = 8
TS = 4
NS = B * TS
T = NP + NS
HD = 64
KV = 2
GRP = 4
H = 4
NB = NP // P
G4 = 4
WINDOWS = (2, 4, 8, 16)
PAD = 16
SEG = PAD + TS
UX = PAD + NP + B * SEG
SK = P + NS
EPS = 1e-6
NEG = -1e30
LB_FLOOR = 1e-30
LEVELS = (64, 32, 16, 8, 4, 2, 1)
HEAD = 1

U_Q, U_K, U_V, U_U, U_HF, U_HQ, U_HI, U_HG = 0, 4, 5, 6, 10, 14, 18, 22
U_GATE = 26
U_BR = 50
U_O = 62
U_FFN = 70
FI = 4
UNITS = U_FFN + FI * 16
RING = 4
LEAD = 2
UW = 1024
PER_SLOT = [len(range(r, UNITS, RING)) for r in range(RING)]
T_BR, T_O, T_FFN = 50, 74, 82
ACT_READS = T_BR + 8 * FI
DVE_READS = (T_FFN - T_BR) + 8 * FI

C = {}


def _constants():
    cols = []
    at = 0

    def put(name, a):
        nonlocal at
        a = np.asarray(a, np.float32).reshape(P, -1)
        C[name] = (at, a.shape[1])
        at += a.shape[1]
        cols.append(a)

    p = np.arange(P)
    put("ident", np.eye(P))
    put("ones", np.ones((P, P)))
    put("headones", (p[:, None] // HD == p[None, :] // HD))
    perm = np.zeros((P, P))
    for i in range(P):
        if i % HD < HD // 2:
            perm[i + HD // 2, i] = -1.0
        else:
            perm[i - HD // 2, i] = 1.0
    put("perm", perm)
    pos = np.concatenate([np.arange(NP), np.tile(1024 + np.arange(TS), B)]).astype(np.float32)
    inv = np.power(np.float32(10000.0), -np.arange(0, HD, 2, dtype=np.float32) / HD).astype(np.float32)
    ang = (pos[None, :] * inv[p % (HD // 2)][:, None]).astype(np.float32)
    put("cos", np.cos(ang))
    put("sin", np.sin(ang))
    q, k = p[:, None], p[None, :]
    put("mask_prev", np.concatenate([np.where(k > q, 0.0, NEG), np.where(k <= q, 0.0, NEG)], 1))
    t_row, b_row = p % TS, p // 32
    ms = []
    for g in range(2):
        j = np.arange(P)[None, :]
        cache = np.where(j > t_row[:, None], 0.0, NEG)
        n = np.arange(NS)[None, :]
        new = np.where((n // TS == (4 * g + b_row)[:, None]) & (n % TS <= t_row[:, None]), 0.0, NEG)
        ms.append(np.concatenate([cache, new], 1))
    put("mask_samp", np.stack(ms, 1))
    e = np.arange(PAD)
    put("invcnt", np.tile(np.stack([1.0 / np.minimum(w, e + 1) for w in WINDOWS])[None], (P, 1, 1)))
    seg = np.ones(T)
    seg[[0, P]] = 0.0
    seg[NP::TS] = 0.0
    put("seg", np.tile(seg[None], (P, 1)))
    put("bmask", (p[:, None] // TS == np.arange(B)[None, :]))
    put("eps", np.full((P, 1), EPS))
    put("one", np.ones((P, 1)))
    return np.ascontiguousarray(np.concatenate(cols, 1))


def _level_masks():
    s, t = np.arange(P)[:, None], np.arange(P)[None, :]
    ms = [(s // (2 * m) == t // (2 * m)) & (s % (2 * m) < m) & (t % (2 * m) >= m) for m in LEVELS]
    ms.append(s == t)
    return np.ascontiguousarray(np.stack(ms, 1).astype(np.float32)).reshape(P, -1)


PAR = {}
_at = 0
for _name, _n in (("norm_mix", KT), ("norm_ffn", KT), ("qw", 1), ("kw", 1), ("sink", 8), ("sink_s", 1),
                  ("onorm", 1), ("pscale", G4), ("lb", H)):
    PAR[_name] = (_at, _n)
    _at += _n
NPAR_IN = _at
for _name in ("log_lb", "log_om", "om"):
    PAR[_name] = (_at, H)
    _at += H
NPAR = _at

OUT_SHAPES = {
    "y": (P, KT, T), "k_out": (DEPTH, P, T), "v_out": (DEPTH, P, T), "u_out": (DEPTH, P, G4 * UX),
    "sp_out": (DEPTH, P, H, P), "ss_out": (DEPTH, P, B * H, P),
    "kc_out": (DEPTH * B, (P - TS) * P), "vc_out": (DEPTH * B, (P - TS) * P),
}


def build(nc, io):
    _constants()
    ctx = ExitStack()
    with ctx:
        def sb(name, shape, dt=F32):
            return ctx.enter_context(nc.sbuf_tensor(name, shape, dt))

        raw = sb("raw", [P, RING, UW])
        w_hi = sb("w_hi", [P, RING, UW], F32R)
        w_lo = sb("w_lo", [P, RING, UW], F32R)
        x = sb("x", [P, KT, T])
        a_hi = sb("a_hi", [P, KT, T], F32R)
        a_lo = sb("a_lo", [P, KT, T], F32R)
        h_hi = sb("h_hi", [P, KT, T], F32R)
        h_lo = sb("h_lo", [P, KT, T], F32R)
        consts = sb("consts", [P, sum(n for _, n in C.values())])
        lmask = sb("lmask", [P, len(LEVELS) + 1, P], U8)
        params = sb("params", [P, DEPTH, NPAR])
        par = sb("par", [P, NPAR])
        poolw = sb("poolw", [P, G4, P])
        small = sb("small", [P, 164])
        pool_d = sb("pool_d", [P, G4, T])
        HT = H * T
        HT = H * T
        sizes = [("A", 3 * KT * T), ("ZF", HT), ("ZQ", HT), ("ZI", HT), ("ZG", HT), ("R", 5 * HT),
                 ("itok", 3 * 512), ("ktok", 2 * 512), ("AC", 512), ("ktok_s", 512), ("ATs", 128),
                 ("S0", B * H * P)]
        arena = sb("arena", [P, sum(n for _, n in sizes)])
        reg, at = {}, 0
        for name, n in sizes:
            reg[name] = arena[:, at:at + n]
            at += n
        A, ZF, ZQ, ZI, ZG, R, ktok, AC, ATs, S0 = (
            reg[n] for n in ("A", "ZF", "ZQ", "ZI", "ZG", "R", "ktok", "AC", "ATs", "S0"))

        def c(name, rows=slice(0, P)):
            o, n = C[name]
            return consts[rows, o:o + n]

        def pr(name, i=0, n=1):
            o = PAR[name][0] + i
            return par[:, o:o + n]

        def bc(a, n):
            return a.rearrange("p (o m) -> p o m", o=1).to_broadcast([a.shape[0], n, a.shape[1]])

        def bl(a, n):
            return a.rearrange("p (m o) -> p m o", o=1).to_broadcast([a.shape[0], a.shape[1], n])

        def hv(a):
            return a.rearrange("p (h t) -> p h t", t=T)

        gates = A.rearrange("p (n k t) -> p n k t", n=3, k=KT)
        sq = A[:, 0:2 * T].rearrange("p (s t) -> p s t", s=2)
        ssum = A[:, 2 * T:3 * T]
        rstd = A[:, 3 * T:4 * T]
        xn = A[:, 4 * T:12 * T].rearrange("p (k t) -> p k t", k=KT)
        relu = A[:, 12 * T:14 * T].rearrange("p (s t) -> p s t", s=2)
        hsq = A[:, 14 * T:16 * T].rearrange("p (s t) -> p s t", s=2)
        sin_t = A[:, 0:5 * T]
        prob = A[:, 0:3072].rearrange("p (g n) -> p g n", g=6)
        probT = A[:, 3072:6144].rearrange("p (g n) -> p g n", g=6)
        qk = R[:, 0:5 * T]
        qk_rs = R[:, 5 * T:10 * T]
        kcT = R[:, 10 * T:10 * T + B * P].rearrange("p (b s) -> p b s", b=B)
        vc = R[:, 10 * T + B * P:10 * T + 2 * B * P].rearrange("p (b n) -> p b n", b=B)
        tail = R[:, 10 * T + 2 * B * P:5 * HT]
        vz = tail[:, 0:T]
        v_tok = tail[:, T:T + 384].rearrange("p (b n) -> p b n", b=3)
        q_samp = AC[:, 0:256]
        psT = AC[:, 256:512].rearrange("p (g n) -> p g n", g=2)
        p_samp = reg["ktok_s"][:, 0:2 * SK].rearrange("p (g n) -> p g n", g=2)
        pnT = ktok[:, 0:256].rearrange("p (g n) -> p g n", g=2)
        uext = S0[:, 0:G4 * UX].rearrange("p (g n) -> p g n", g=G4)
        wa = S0[:, G4 * UX:2 * G4 * UX].rearrange("p (g n) -> p g n", g=G4)
        first = S0[:, 2 * G4 * UX:2 * G4 * UX + G4 * PAD].rearrange("p (g n) -> p g n", g=G4)
        wb = reg["itok"][:, 0:3 * UX].rearrange("p (g n) -> p g n", g=3)
        wsum = [wa[:, 0], wb[:, 0], wa[:, 2], wb[:, 2]]
        KK, GG, D0, X0, X1 = (R[:, i * HT:(i + 1) * HT] for i in range(5))

        itok = reg["itok"].rearrange("p (b h n) -> p b h n", b=3, h=H)
        ktok4 = ktok.rearrange("p (b h n) -> p b h n", b=NB, h=H)
        ktok_s = reg["ktok_s"].rearrange("p (h n) -> p h n", h=H)
        AT = ktok.rearrange("p (b h t) -> p b h t", b=NB, h=H)
        ACv = AC.rearrange("p (h t) -> p h t", h=H)
        ATsv = ATs.rearrange("p (h t) -> p h t", h=H)
        S0v = S0.rearrange("p (b h n) -> p b h n", b=B, h=H)
        D1 = pool_d

        PZ = [ctx.enter_context(nc.psum_tensor(f"pz{i}", [P, 512], F32)) for i in range(4)]
        pm = ctx.enter_context(nc.psum_tensor("pm", [P, 4, 512], F32))
        PM = [pm[:, i, :] for i in range(4)]

        def cols(o, n):
            return small[:, o:o + n]
        mx, negm, sm, se, es_, den, rec = (cols(18 * i, 18) for i in range(7))
        ep, es = cols(126, H), cols(130, B * H)

        made = {}

        class Sems:
            def __getitem__(self, name):
                if name not in made:
                    made[name] = ctx.enter_context(nc.semaphore(name))
                return made[name]
        s = Sems()
        ld = [s[f"raw_landed{r}"] for r in range(RING)]

        class Chain:

            def __init__(self, eng, name, per_layer):
                self.eng, self.sem, self.per_layer, self.base, self.k = eng, s[name], per_layer, 0, 0

            def layer(self, base):
                self.base, self.k = base, 0

            def __call__(self, ins):
                self.k += 1
                ins.then_inc(self.sem, 1)
                self.eng.wait_ge(self.sem, self.base + self.k)

            def close(self):
                assert self.k == self.per_layer, (self.sem, self.k)

        def slot_landed(u, l, i=0):
            return (l * PER_SLOT[u % RING] + (u // RING + 1) + i * (16 // RING)) * 16

        def gate_tile(t):
            return gates[:, 2 - (t - U_GATE) // KT, (t - U_GATE) % KT]

        def level_views(a, m):
            w = T if m <= 2 else NP
            v = hv(a)[:, :, 0:w].rearrange("p h (a e s) -> p h a e s", e=2, s=m)
            return v[:, :, :, 0, :], v[:, :, :, 1, :]

        def samp(a):
            return a.rearrange("p (b t) -> p b t", t=TS)

        def samp_out(h, kv):
            rows = slice(kv * HD, (kv + 1) * HD)
            o = h[rows, 4:8, NP:T].rearrange("p j (b t) -> p b j t", t=TS)
            z = PM[1][rows, 0:256].rearrange("p (b k j t) -> p b k j t", b=B, k=KV, j=GRP)[:, :, kv]
            return o, z

        block = ctx.enter_context(nc.Block())

        @block.sync
        def _(sp):
            sp.dma_start(x[:], io["x_in"]).then_inc(s["x_landed"], 16)
            sp.dma_start(params[:, :, 0:NPAR_IN], io["params"]).then_inc(s["params_landed"], 16)
            sp.dma_start(consts[:], io["consts"]).then_inc(s["consts_landed"], 16)
            sp.dma_start(A[:, 8 * P * 4:8 * P * 5], io["lmask"]).then_inc(s["lmask_landed"], 16)

            def load(l, u, r, used):
                sp.wait_ge(s["w_lo"], used + HEAD)
                sp.dma_start(raw[:, r], io["w"][l, bass.ds(u, 1)].rearrange("o p n -> (o p) n")).then_inc(ld[r], 16)

            with sp.Fori(0, DEPTH) as l:
                for u in range(RING):
                    load(l, u, u, l * UNITS)
                sp.wait_ge(s["snew_read"], 4 * l + HEAD)
                sp.sem_inc(s["sp_passed"], 1)
                sp.wait_ge(s["oa_lo"], l + HEAD)
                sp.sem_inc(s["sp_passed"], 1)
                sp.dma_start(kcT, io["kcT"][l]).then_inc(s["cache_landed"], 16)
                sp.dma_start(vc, io["vc"][l]).then_inc(s["cache_landed"], 16)
                sp.wait_ge(s["pool_y"], l + HEAD)
                sp.sem_inc(s["sp_passed"], 1)
                sp.dma_start(poolw[:], io["pool_w"][l]).then_inc(s["poolw_landed"], 16)
                sp.wait_ge(s["s0_free"], l + HEAD)
                sp.sem_inc(s["sp_passed"], 1)
                sp.dma_start(uext[:, :, PAD + NP:], io["pool_state"][l]).then_inc(s["ustate_landed"], 16)
                with sp.Fori(0, 6) as i:
                    for r in range(RING):
                        load(l, i * RING + (RING + r), r, l * UNITS + i * RING + (r + 1))
                sp.wait_ge(s["u_out"], (l + 1) * 16)
                sp.sem_inc(s["sp_passed"], 1)
                sp.wait_ge(s["pool_d"], (l + 1) * 8)
                sp.sem_inc(s["sp_passed"], 1)
                sp.wait_ge(s["pool_first"], (l + 1) * 2)
                sp.sem_inc(s["sp_passed"], 1)
                sp.dma_start(S0, io["s0"][l]).then_inc(s["s0_landed"], 16)
                with sp.Fori(0, 26) as i:
                    for r in range(RING):
                        load(l, i * RING + (28 + r), r, l * UNITS + i * RING + (25 + r))
                for u in (132, 133):
                    load(l, u, u % RING, l * UNITS + (u - RING + 1))
            sp.wait_ge(s["z_read_dve"], DEPTH * DVE_READS + HEAD)
            sp.dma_start(io["y"], x[:]).then_inc(s["y_out"], 16)
            sp.wait_ge(s["y_out"], 16)

        @block.tensor
        def _(pe):
            def mm(out, a, b, start=True, stop=True, **kw):
                return nc.tensor.matmul(out, a, b, start=start, stop=stop, **kw)

            def product(outs, u, wv, rhs_hi, rhs_lo, kk, have=None):
                for n, out in enumerate(outs):
                    for k in range(kk):
                        if have is not None and n == 0:
                            have(k)
                        hi = w_hi[:, u % RING].rearrange("p (k c) -> p k c", k=kk)[:, k, n * P:(n + 1) * P]
                        lo = w_lo[:, u % RING].rearrange("p (k c) -> p k c", k=kk)[:, k, n * P:(n + 1) * P]
                        mm(out, hi, rhs_hi(k), start=k == 0, stop=False)
                        mm(out, hi, rhs_lo(k), start=False, stop=False)
                        last = mm(out, lo, rhs_hi(k), start=False, stop=k == kk - 1)
                    if n < len(outs) - 1:
                        last.then_inc(s["half_done"], 1)
                last.then_inc(s["unit_done"], 1)

            def unit(l, u):
                pe.wait_ge(s["w_lo"], l * UNITS + (u + 1) + HEAD)
                if u < U_BR:
                    tiles = [u]
                elif u < U_O:
                    tiles = [T_BR + 2 * (u - U_BR), T_BR + 2 * (u - U_BR) + 1]
                else:
                    tiles = [T_O + u - U_O]
                t4 = tiles[-1] - 4
                if t4 < 0:
                    pe.wait_ge(s["z_read_dve"], l * DVE_READS + HEAD)
                elif t4 < T_BR:
                    pe.wait_ge(s["z_read_act"], l * ACT_READS + (t4 + 1))
                else:
                    if tiles[0] - 4 < T_BR:
                        pe.wait_ge(s["z_read_act"], l * ACT_READS + T_BR)
                    pe.wait_ge(s["z_read_dve"], l * DVE_READS + (t4 - T_BR + 1) + HEAD)
                outs = [PZ[t % 4][:, 0:T] for t in tiles]
                if u < U_BR:
                    have = (lambda k: pe.wait_ge(s["a_lo"], l * 16 + (k + 1))) if u == 0 else None
                    product(outs, u, 1, lambda k: a_hi[:, k], lambda k: a_lo[:, k], KT, have)
                elif u < U_O:
                    n, half = 2 - (u - U_BR) // 4, (u - U_BR) % 4
                    if half == 0:
                        if n == 2:
                            pe.wait_ge(s["oc_lo"], (l + 1) * G4)
                        elif n == 1:
                            pe.wait_ge(s["ob_lo"], (l + 1) * 4)
                        else:
                            pe.wait_ge(s["oa_lo"], l + 1 + HEAD)
                    hi, lo, o = ((a_hi, a_lo, 0), (h_hi, h_lo, 4), (h_hi, h_lo, 0))[n]
                    product(outs, u, 2, lambda k: hi[:, o + k], lambda k: lo[:, o + k], 4)
                else:
                    have = (lambda k: pe.wait_ge(s["m_lo"], l * KT + (k + 1))) if u == U_O else None
                    product(outs, u, 1, lambda k: h_hi[:, k], lambda k: h_lo[:, k], KT, have)

            def norm_sum(n):
                pe.wait_ge(s["ssum"], n * KT + HEAD)
                mm(PM[3][:, 0:T], c("ones"), ssum).then_inc(s["nsum"], 1)

            def attention(l, u):
                kvr = [slice(0, HD), slice(HD, P)]
                qkv = qk.rearrange("p (j t) -> p j t", t=T)
                if u == 5:
                    pe.wait_ge(s["qk_sq"], l + 1)
                    for i in range(3):
                        last = mm(PM[i][:, 0:480], c("headones"), qk_rs[:, i * 480:(i + 1) * 480])
                    last.then_inc(s["qk_ss"], 1)
                if u == 6:
                    pe.wait_ge(s["z_read_act"], l * ACT_READS + (U_V + 1))
                    pe.wait_ge(s["rstd"], 2 * l + 1)
                    for i, (o, n) in enumerate(((0, P), (P, P), (NP, NS))):
                        last = nc.tensor.transpose(PM[3][0:n, i * P:(i + 1) * P], vz[:, o:o + n], c("ident"))
                    last.then_inc(s["v_tr"], 1)
                if u == 8:
                    pe.wait_ge(s["qk_norm"], 2 * l + 2)
                    pe.wait_ge(s["v_tok"], 2 * l + 2)
                    for j in range(4):
                        last = mm(PM[j][:, 0:T], c("perm"), qkv[:, j])
                    last.then_inc(s["qk_rot"], 1)
                if u == 9:
                    pe.wait_ge(s["rot_read"], 2 * l + 1)
                    mm(PM[0][:, 0:T], c("perm"), qkv[:, 4]).then_inc(s["qk_rot"], 1)
                if u == 11:
                    pe.wait_ge(s["qk_rope"], l + 1)
                if u in (11, 13):
                    for g in ((0, 1, 2, 3) if u == 11 else (4, 5)):
                        if g >= 4:
                            pe.wait_ge(s["score_read"], l * 7 + (g - 3))
                        if g < 2:
                            for j in range(GRP):
                                last = mm(PM[g][:, j * P:(j + 1) * P], qkv[kvr[g], j, 0:P], qkv[kvr[g], 4, 0:P])
                        else:
                            kv, j0 = (g - 2) // 2, 2 * (g % 2)
                            for a in range(2):
                                last = mm(PM[g % 4][:, a * NP:(a + 1) * NP], qkv[kvr[kv], j0 + a, P:NP],
                                          qkv[kvr[kv], 4, 0:NP])
                        last.then_inc(s["score"], 1)
                if u == 14:
                    pe.wait_ge(s["score_read"], l * 7 + 3)
                    pe.wait_ge(s["q_samp"], 2 * l + 2)
                    pe.wait_ge(s["cache_landed"], 32 * (l + 1))
                    for g in range(2):
                        for b in range(4):
                            mm(PM[2][32 * b:32 * b + 32, g * SK:g * SK + P],
                               q_samp[:, (4 * g + b) * 32:(4 * g + b + 1) * 32], kcT[:, 4 * g + b])
                        last = mm(PM[2][:, g * SK + P:(g + 1) * SK], q_samp[:, g * P:(g + 1) * P],
                                  qkv[:, 4, NP:T])
                    last.then_inc(s["score"], 1)
                if u == 20:
                    pe.wait_ge(s["oc_lo"], (l + 1) * G4)
                if u in (20, 21, 22):
                    for tg in {20: (0, 1), 21: (2, 3), 22: (4, 5)}[u]:
                        if tg < 2:
                            pe.wait_ge(s["prob_n"], l * 7 + (tg + 1))
                            src = [prob[:, tg, j * P:(j + 1) * P] for j in range(GRP)]
                        else:
                            kv, a = (tg - 2) // 2, tg % 2
                            pe.wait_ge(s["prob_n"], l * 7 + (4 + 2 * kv))
                            src = [prob[:, 2 + 2 * kv + j // 2, (j % 2) * NP + a * P:(j % 2) * NP + (a + 1) * P]
                                   for j in range(GRP)]
                        if tg >= 4:
                            pe.wait_ge(s["probT"], l * 8 + (tg - 3))
                        for j in range(GRP):
                            last = nc.tensor.transpose(PM[tg % 4][:, j * P:(j + 1) * P], src[j], c("ident"))
                        last.then_inc(s["prob_tr"], 1)
                if u == 22:
                    pe.wait_ge(s["prob_n"], l * 7 + 7)
                    pe.wait_ge(s["probT"], l * 8 + 3)
                    for g in range(2):
                        nc.tensor.transpose(PM[2][:, g * P:(g + 1) * P], p_samp[:, g, 0:P], c("ident"))
                        last = nc.tensor.transpose(PM[2][0:NS, (2 + g) * P:(3 + g) * P], p_samp[:, g, P:SK],
                                                   c("ident"))
                    last.then_inc(s["prob_tr"], 1)
                if u == 24:
                    pe.wait_ge(s["probT"], l * 8 + 8)
                    for kv in range(KV):
                        last = mm(PM[3][kvr[kv], :], v_tok[:, 0, kvr[kv]], probT[:, kv])
                    last.then_inc(s["pv"], 1)
                    for kv in range(KV):
                        mm(PM[0][kvr[kv], :], v_tok[:, 0, kvr[kv]], probT[:, 2 + 2 * kv], stop=False)
                        last = mm(PM[0][kvr[kv], :], v_tok[:, 1, kvr[kv]], probT[:, 3 + 2 * kv], start=False)
                    last.then_inc(s["pv"], 1)
                    mm(PM[1][:, 0:2 * P], v_tok[0:NS, 2], pnT[0:NS], skip_group_check=True)
                    for b in range(B):
                        last = mm(PM[1][:, b * 32:(b + 1) * 32], vc[:, b],
                                  psT[:, b // 4, (b % 4) * 32:(b % 4 + 1) * 32], start=False,
                                  skip_group_check=True)
                    last.then_inc(s["pv"], 1)

            def pooling(l, u):
                if u == 17:
                    pe.wait_ge(s["pool_d"], (l + 1) * 8)
                    pe.wait_ge(s["pool_first"], (l + 1) * 2)
                    pe.wait_ge(s["poolw_landed"], (l + 1) * 16)
                    pe.wait_ge(s["score_read"], (l + 1) * 7)
                    for g in range(G4):
                        last = mm(PM[g][:, 0:T], poolw[:, g], pool_d[:, g])
                    last.then_inc(s["pool_y"], 1)

            def diag_sample(xk, xq, bank):
                for h in range(H):
                    last = mm(bank[0:NS, h * NS:(h + 1) * NS], hv(xk)[:, h, NP:T], hv(xq)[:, h, NP:T])
                return last

            def hgrn(l, u):
                if u == 28:
                    pe.wait_ge(s["ob_lo"], (l + 1) * 4)
                    pe.wait_ge(s["z_read_act"], l * ACT_READS + (U_HI + 4))
                    for h in range(H):
                        for n in range(3):
                            w = P if n < 2 else NS
                            last = nc.tensor.transpose(PM[n][0:w, h * P:(h + 1) * P],
                                                       hv(ZI)[:, h, n * P:n * P + w], c("ident"))
                    last.then_inc(s["i_tr"], 1)
                if u == 32:
                    pe.wait_ge(s["KE"], l + 1)
                    pe.wait_ge(s["QE"], l + 1)
                    pe.wait_ge(s["itok"], 2 * l + 2)
                    for h in range(H):
                        for n in range(3):
                            w = P if n < 2 else NS
                            last = nc.tensor.transpose(PM[n][0:w, h * P:(h + 1) * P],
                                                       hv(X1)[:, h, n * P:n * P + w], c("ident"))
                    last.then_inc(s["k_tr"], 1)
                    for h in range(H):
                        last = mm(PM[3][:, h * P:(h + 1) * P], hv(X1)[:, h, 0:P], hv(ZF)[:, h, P:NP])
                    last.then_inc(s["cross"], 1)
                if u == 34:
                    pe.wait_ge(s["ktok"], 2 * l + 2)
                    for n in range(NB):
                        for h in range(H):
                            last = mm(PM[n][:, h * P:(h + 1) * P], ktok4[:, n, h], itok[:, n, h])
                    last.then_inc(s["sfin"], 1)
                    pe.wait_ge(s["AC"], l + 1)
                    for n in range(NB):
                        for h in range(H):
                            last = mm(PM[2 + n][:, h * P:(h + 1) * P], hv(KK)[:, h, n * P:(n + 1) * P],
                                      hv(ZQ)[:, h, n * P:(n + 1) * P])
                    last.then_inc(s["level_mm"], 1)
                if u == 36:
                    pe.wait_ge(s["level_read"], 11 * l + 1)
                    diag_sample(KK, ZQ, PM[2]).then_inc(s["level_mm"], 1)
                if 36 <= u <= 48 and u % 2 == 0:
                    i = (u - 36) // 2
                    X = (X0, X1)[i % 2]
                    b0 = 2 * (i % 2)
                    pe.wait_ge(s["level_x"], 14 * l + 2 * (i + 1))
                    if i == 0:
                        pe.wait_ge(s["sfin_read"], l + 1)
                    elif i == 1:
                        pe.wait_ge(s["level_read"], 11 * l + 2)
                    elif i < 6:
                        pe.wait_ge(s["level_read"], 11 * l + (i + 1))
                    else:
                        pe.wait_ge(s["level_read"], 11 * l + 9)
                    for n in range(NB):
                        for h in range(H):
                            xs = hv(X)[:, h, n * P:(n + 1) * P]
                            last = mm(PM[b0 + n][:, h * P:(h + 1) * P], xs, xs)
                    last.then_inc(s["level_mm"], 1)
                    if i == 5:
                        pe.wait_ge(s["level_read"], 11 * l + 7)
                        diag_sample(X, X, PM[0]).then_inc(s["level_mm"], 1)
                    if i == 6:
                        pe.wait_ge(s["level_read"], 11 * l + 8)
                        diag_sample(X, X, PM[2]).then_inc(s["level_mm"], 1)
                if u == 50:
                    pe.wait_ge(s["level_read"], 11 * l + 11)
                    pe.wait_ge(s["s0_landed"], 16 * (l + 1))
                    for h in range(H):
                        last = mm(PM[3][:, h * P:(h + 1) * P], itok[:, 0, h], AT[:, 0, h])
                    last.then_inc(s["o_ps"], 1)
                    for h in range(H):
                        mm(PM[0][:, h * P:(h + 1) * P], itok[:, 0, h], ACv[:, h], stop=False)
                        last = mm(PM[0][:, h * P:(h + 1) * P], itok[:, 1, h], AT[:, 1, h], start=False)
                    last.then_inc(s["o_ps"], 1)
                    for h in range(H):
                        mm(PM[1][:, h * NS:(h + 1) * NS], itok[0:NS, 2, h], ATsv[0:NS, h],
                           skip_group_check=True)
                        for b in range(B):
                            o = h * NS + b * TS
                            last = mm(PM[1][:, o:o + TS], S0v[:, b, h], hv(ZF)[:, h, NP + b * TS:NP + (b + 1) * TS],
                                      start=False, skip_group_check=True)
                    last.then_inc(s["o_ps"], 1)
                if u == 52:
                    pe.wait_ge(s["o_sq"], l + 1)
                    for i in range(3):
                        last = mm(PM[i][:, 0:384], c("ones"), D0[:, i * 384:(i + 1) * 384])
                    last.then_inc(s["o_ss"], 1)
                if u in (57, 59):
                    pe.wait_ge(s["o_rstd"], l + 1)
                    for h in ((0, 1) if u == 57 else (2, 3)):
                        pe.wait_ge(s["imask"], 4 * l + (h + 1))
                        if h >= 2:
                            pe.wait_ge(s["snew_read"], 4 * l + (h - 1) + HEAD)
                        im = (KK, GG, X1, ZF)[h]
                        for half in range(2):
                            last = mm(PM[2 * (h % 2) + half], ktok_s[0:NS, h], im[0:NS, half * 512:(half + 1) * 512])
                        last.then_inc(s["snew"], 1)

            for name in ("unit_done", "nsum", "pool_y"):
                pe.sem_inc(s[name], HEAD)
            pe.wait_ge(s["consts_landed"], 16)
            with pe.Fori(0, DEPTH) as l:
                norm_sum(2 * l + 1)
                for u in range(U_FFN):
                    unit(l, u)
                    attention(l, u)
                    pooling(l, u)
                    hgrn(l, u)
                pe.wait_ge(s["snew_read"], 4 * l + 4 + HEAD)
                norm_sum(2 * l + 2)
                with pe.Fori(0, FI) as i:
                    for j in range(16):
                        u = U_FFN + j
                        pe.wait_ge(s["w_lo"], l * UNITS + i * 16 + (u + 1) + HEAD)
                        if j < 4:
                            pe.wait_ge(s["z_read_dve"], l * DVE_READS + i * 8 + (T_FFN - T_BR - 3 + j) + HEAD)
                        elif j < 12:
                            pe.wait_ge(s["z_read_act"], l * ACT_READS + i * 8 + (T_BR + j - 3))
                        else:
                            pe.wait_ge(s["z_read_dve"], l * DVE_READS + i * 8 + (T_FFN - T_BR + j - 11) + HEAD)
                        out = [PZ[(T_FFN + j) % 4][:, 0:T]]
                        if j < 8:
                            have = (lambda k: pe.wait_ge(s["a_lo"], l * 16 + (9 + k))) if j == 0 else None
                            product(out, u, 1, lambda k: a_hi[:, k], lambda k: a_lo[:, k], KT, have)
                        else:
                            have = (lambda k: pe.wait_ge(s["f_lo"], l * 8 * FI + i * 8 + (k + 1) + HEAD)) if j == 8 else None
                            product(out, u, 1, lambda k: h_hi[:, k], lambda k: h_lo[:, k], KT, have)

        @block.scalar
        def _(act):
            chain = Chain(act, "act_chain", 6)
            act_fn = nc.scalar.activation
            one, eps = c("one"), c("eps")

            def split(l, u, i=0):
                r = u % RING
                act.wait_ge(ld[r], slot_landed(u, l, i))
                act.wait_ge(s["unit_done"], (l * UNITS if u < RING else l * UNITS + i * 16 + (u - RING + 1)) + HEAD)
                act_fn(w_hi[:, r], raw[:, r], ACT.Copy).then_inc(s["w_hi"], 1)

            def squares(n, j, ready):
                act.wait_ge(s["z_read_dve"], ready + HEAD)
                act.wait_ge(s["ssum"], (n - 1) * KT + max(j - 1, 0) + HEAD)
                act_fn(sq[:, j % 2], x[:, j], ACT.Square).then_inc(s["x_sq"], 1)

            def norm(n):
                act.wait_ge(s["nsum"], n + HEAD)
                chain(act_fn(rstd, PM[3][:, 0:T], ACT.Ln, bias=eps, scale=1.0 / D_MODEL))
                act_fn(rstd, rstd, ACT.Exp, scale=-0.5).then_inc(s["rstd"], 1)
                for j in range(KT):
                    act.wait_ge(s["xn"], (n - 1) * KT + (j + 1))
                    act_fn(a_hi[:, j], xn[:, j], ACT.Copy).then_inc(s["a_hi"], 1)

            def read_tile(l, t):
                act.wait_ge(s["unit_done"], l * UNITS + (t + 1) + HEAD)
                z = PZ[t % 4][:, 0:T]
                if U_U <= t < U_HF:
                    g = t - U_U
                    if g == 0:
                        act.wait_ge(s["s0_free"], l + HEAD)
                    act_fn(uext[:, g, PAD:PAD + NP], z[:, 0:NP], ACT.Copy)
                    out = uext[:, g, PAD + NP:].rearrange("p (b n) -> p b n", n=SEG)[:, :, PAD:]
                    if g == 0:
                        act.wait_ge(s["ustate_landed"], 16 * (l + 1))
                    act_fn(out, samp(z[:, NP:T]), ACT.Copy).then_inc(s["z_read_act"], 1)
                    return
                if t <= U_K:
                    out = qk[:, t * T:(t + 1) * T]
                elif t == U_V:
                    out = vz
                elif t < U_GATE:
                    base, first_u = ((ZF, U_HF), (ZQ, U_HQ), (ZI, U_HI), (ZG, U_HG))[(t - U_HF) // 4]
                    out = hv(base)[:, t - first_u]
                else:
                    out = gate_tile(t)
                act_fn(out, z, ACT.Copy).then_inc(s["z_read_act"], 1)

            def attention(l, u):
                if u == 4:
                    act.wait_ge(s["z_read_act"], l * ACT_READS + (U_K + 1))
                    act_fn(qk_rs, qk, ACT.Square).then_inc(s["qk_sq"], 1)
                if u == 6:
                    act.wait_ge(s["qk_ss"], l + 1)
                    r3 = qk_rs.rearrange("p (b n) -> p b n", b=3)
                    chain(act_fn(r3, pm[:, 0:3, 0:480], ACT.Ln, bias=eps, scale=1.0 / HD))
                    act_fn(qk_rs, qk_rs, ACT.Exp, scale=-0.5).then_inc(s["qk_rstd"], 1)
                if u == 7:
                    act.wait_ge(s["v_tr"], l + 1)
                    act_fn(v_tok[:, 0:2], PM[3][:, 0:256].rearrange("p (b n) -> p b n", b=2),
                           ACT.Copy).then_inc(s["v_tok"], 1)
                    act_fn(v_tok[0:NS, 2], PM[3][0:NS, 256:384], ACT.Copy).then_inc(s["v_tok"], 1)
                if u == 16:
                    act.wait_ge(s["negm"], l + 1)
                    act_fn(es_, se, ACT.Exp).then_inc(s["sink_e"], 1)
                for g in {16: (0, 1), 17: (2, 3, 4, 5, 6)}.get(u, ()):
                    heads = GRP if g < 2 else 2
                    for a in range(heads):
                        col = g * 4 + a if g < 2 else 8 + 2 * (g - 2) + a
                        if g < 6:
                            w = 512 // heads
                            pg = prob[:, g, a * w:(a + 1) * w]
                        else:
                            pg = p_samp[:, a]
                        last = act_fn(pg, pg, ACT.Exp, bias=negm[:, col:col + 1], accum_out=sm[:, col:col + 1])
                        last.then_inc(s["prob_e"], 1)
                for tg in {21: (0, 1), 22: (2, 3), 23: (4, 5)}.get(u, ()):
                    act.wait_ge(s["prob_tr"], 7 * l + (tg + 1))
                    act_fn(probT[:, tg], PM[tg % 4], ACT.Copy).then_inc(s["probT"], 1)
                if u == 23:
                    act.wait_ge(s["prob_tr"], 7 * l + 7)
                    act_fn(psT, PM[2][:, 0:256].rearrange("p (g n) -> p g n", g=2), ACT.Copy).then_inc(s["probT"], 1)
                    act_fn(pnT[0:NS], PM[2][0:NS, 256:512].rearrange("p (g n) -> p g n", g=2),
                           ACT.Copy).then_inc(s["probT"], 1)
                if u == 25:
                    for n in range(2):
                        act.wait_ge(s["pv"], 3 * l + (n + 1))
                        act_fn(h_hi[:, 4:8, n * P:(n + 1) * P], PM[3 - 3 * n].rearrange("p (j t) -> p j t", j=4),
                               ACT.Copy).then_inc(s["ob_hi"], 1)
                    act.wait_ge(s["pv"], 3 * l + 3)
                    for kv in range(KV):
                        o, z = samp_out(h_hi, kv)
                        act_fn(o, z, ACT.Copy).then_inc(s["ob_hi"], 1)

            def pooling(l, u):
                if u == 18:
                    act.wait_ge(s["pool_y"], l + 1 + HEAD)
                    for g in range(G4):
                        act_fn(h_hi[:, g], PM[g][:, 0:T], ACT.Copy, scale=pr("pscale", g)).then_inc(s["oc_hi"], 1)

            def hgrn(l, u):
                if u == 26:
                    act.wait_ge(s["kv_out"], 32 * (l + 1))
                    act.wait_ge(s["ob_lo"], 4 * (l + 1))
                    act.wait_ge(s["z_read_act"], l * ACT_READS + (U_HG + 4))
                    act_fn(D0, ZQ, ACT.Sigmoid).then_inc(s["sig"], 1)
                    act_fn(KK, ZF, ACT.Sigmoid, scale=-1.0).then_inc(s["sig"], 1)
                    act_fn(D1[:].rearrange("p h t -> p (h t)"), ZG, ACT.Sigmoid).then_inc(s["sig"], 1)
                if u == 27:
                    act.wait_ge(s["hz_abs"], l + 1)
                    chain(act_fn(X0, X0, ACT.Exp, scale=-1.0))
                    act_fn(X0, X0, ACT.Ln, bias=one).then_inc(s["hz_ln1"], 1)
                if u == 29:
                    act.wait_ge(s["i_tr"], l + 1)
                    act_fn(itok[:, 0:2], pm[:, 0:2].rearrange("p b (h n) -> p b h n", h=H),
                           ACT.Copy).then_inc(s["itok"], 1)
                    act_fn(itok[0:NS, 2], PM[2][0:NS].rearrange("p (h n) -> p h n", h=H),
                           ACT.Copy).then_inc(s["itok"], 1)
                    act.wait_ge(s["hz_dif"], l + 1)
                    chain(act_fn(D0, D0, ACT.Exp))
                    act_fn(D0, D0, ACT.Ln, bias=one).then_inc(s["hz_ln2"], 1)
                if u == 30:
                    act.wait_ge(s["end_g"], 2 * l + 2)
                    act_fn(X0, GG, ACT.Exp).then_inc(s["E0"], 1)
                    d1 = D1[:].rearrange("p h t -> p (h t)")
                    act_fn(d1, d1, ACT.Exp).then_inc(s["E1"], 1)
                if u == 33:
                    act.wait_ge(s["k_tr"], l + 1)
                    act_fn(ktok4, pm[:, 0:2].rearrange("p b (h n) -> p b h n", h=H), ACT.Copy).then_inc(s["ktok"], 1)
                    act_fn(ktok_s[0:NS], PM[2][0:NS].rearrange("p (h n) -> p h n", h=H),
                           ACT.Copy).then_inc(s["ktok"], 1)
                    act.wait_ge(s["cross"], l + 1)
                    act_fn(AC, PM[3], ACT.Copy).then_inc(s["AC"], 1)
                if 35 <= u <= 47 and u % 2:
                    i = (u - 35) // 2
                    D = (hv(D0), D1)[i % 2]
                    w = T if LEVELS[i] <= 2 else NP
                    act.wait_ge(s["level_d"], 14 * l + 2 * (i + 1))
                    act_fn(D[:, :, 0:w], D[:, :, 0:w], ACT.Exp).then_inc(s["level_e"], 1)
                if u == 49:
                    act.wait_ge(s["z_read_act"], l * ACT_READS + T_BR)
                    for n in (2, 1, 0):
                        act_fn(gates[:, n], gates[:, n], ACT.Sigmoid).then_inc(s["gate"], 1)
                if u == 51:
                    act.wait_ge(s["sp_out"], 16 * (l + 1))
                    for n in range(2):
                        act.wait_ge(s["o_ps"], 3 * l + (n + 1))
                        act_fn(hv(ZI)[:, :, n * P:(n + 1) * P], PM[3 - 3 * n].rearrange("p (h t) -> p h t", h=H),
                               ACT.Copy).then_inc(s["o_sb"], 1)
                    act.wait_ge(s["o_ps"], 3 * l + 3)
                    act_fn(hv(ZI)[:, :, NP:T], PM[1][:, 0:H * NS].rearrange("p (h t) -> p h t", h=H),
                           ACT.Copy).then_inc(s["o_sb"], 1)
                    act.wait_ge(s["o_sb"], 3 * l + 3)
                    act_fn(D0, ZI, ACT.Square).then_inc(s["o_sq"], 1)
                if u == 53:
                    act.wait_ge(s["o_ss"], l + 1)
                    d1 = D1[:].rearrange("p h t -> p (h t)")
                    chain(act_fn(d1.rearrange("p (b n) -> p b n", b=3), pm[:, 0:3, 0:384], ACT.Ln, bias=eps,
                                 scale=1.0 / P))
                    act_fn(d1, d1, ACT.Exp, scale=-0.5).then_inc(s["o_rstd"], 1)
                if u == 55:
                    act.wait_ge(s["oa"], l + 1)
                    act_fn(a_hi[:, 0:4], hv(X0), ACT.Copy).then_inc(s["oa_hi"], 1)

            def mlp(l, i, last):
                for j in range(16):
                    if j < 8:
                        act.wait_ge(s["unit_done"], l * UNITS + i * 16 + (U_FFN + j + 1) + HEAD)
                        act.wait_ge(s["hsq"], l * 8 * FI + i * 8 + max(j - 1, 0) + HEAD)
                        act_fn(relu[:, j % 2], PZ[(T_FFN + j) % 4][:, 0:T], ACT.Relu).then_inc(s["z_read_act"], 1)
                    if j + LEAD < 16 or not last:
                        split(l, U_FFN + j + LEAD, i)
                    if 1 <= j < 9:
                        act.wait_ge(s["hsq"], l * 8 * FI + i * 8 + j + HEAD)
                        act_fn(h_hi[:, j - 1], hsq[:, (j - 1) % 2], ACT.Copy).then_inc(s["f_hi"], 1)
                    if last and j >= 8:
                        squares(2 * l + 3, j - 8, l * DVE_READS + (DVE_READS - 15 + j))

            act.wait_ge(s["prep_v"], 1)
            act_fn(small[:, 0:2 * H], small[:, 0:2 * H], ACT.Exp).then_inc(s["prep_a"], 1)
            act.wait_ge(s["prep_v"], 2)
            act_fn(small[:, 32:56], small[:, 32:56], ACT.Ln).then_inc(s["prep_a"], 1)
            act.wait_ge(s["x_landed"], 16)
            act.wait_ge(s["consts_landed"], 16)
            for j in range(KT):
                squares(1, j, 0)
            with act.Fori(0, DEPTH) as l:
                chain.layer(l * chain.per_layer)
                split(l, 0)
                split(l, 1)
                norm(2 * l + 1)
                for u in range(U_FFN):
                    if u < U_BR:
                        read_tile(l, u)
                    split(l, u + LEAD)
                    if u >= U_O:
                        squares(2 * l + 2, u - U_O, l * DVE_READS + (T_O - T_BR + u - U_O + 1))
                    if U_BR + 8 <= u < U_O:
                        for d in (2 * (u - U_BR - 8), 2 * (u - U_BR - 8) + 1):
                            act.wait_ge(s["merged"], l * KT + (d + 1))
                            act_fn(h_hi[:, d], gates[:, 2, d], ACT.Copy).then_inc(s["m_hi"], 1)
                    attention(l, u)
                    pooling(l, u)
                    hgrn(l, u)
                norm(2 * l + 2)
                with act.Fori(0, FI - 1) as i:
                    mlp(l, i, False)
                mlp(l, FI - 1, True)
                chain.close()

        @block.vector
        def _(dve):
            chain = Chain(dve, "dve_chain", 0)
            tt, ts_, stt = nc.vector.tensor_tensor, nc.vector.tensor_scalar, nc.vector.scalar_tensor_tensor
            f = lambda a: a.bitcast(F32)

            def split(l, u, i=0):
                dve.wait_ge(s["w_hi"], l * UNITS + i * 16 + (u + 1))
                r = u % RING
                tt(w_lo[:, r], raw[:, r], f(w_hi[:, r]), ALU.subtract).then_inc(s["w_lo"], 1)

            def add_square(n, j):
                dve.wait_ge(s["x_sq"], (n - 1) * KT + (j + 1))
                if j == 0:
                    dve.wait_ge(s["nsum"], n - 1 + HEAD)
                    nc.vector.tensor_copy(ssum, sq[:, 0]).then_inc(s["ssum"], 1)
                else:
                    dve.wait_ge(s["ssum"], (n - 1) * KT + j + HEAD)
                    tt(ssum, ssum, sq[:, j % 2], ALU.add).then_inc(s["ssum"], 1)

            def norm(n, w):
                dve.wait_ge(s["rstd"], n)
                for j in range(KT + 1):
                    if j < KT:
                        stt(xn[:, j], x[:, j], pr(w, j), rstd, ALU.mult, ALU.mult).then_inc(s["xn"], 1)
                    if j > 0:
                        dve.wait_ge(s["a_hi"], (n - 1) * KT + j)
                        tt(a_lo[:, j - 1], xn[:, j - 1], f(a_hi[:, j - 1]), ALU.subtract).then_inc(s["a_lo"], 1)

            def add_to_x(l, j, z, unit_done):
                dve.wait_ge(s["unit_done"], unit_done + HEAD)
                tt(x[:, j], x[:, j], z[:, 0:T], ALU.add).then_inc(s["z_read_dve"], 1)

            def attention(l, u):
                if u == 7:
                    dve.wait_ge(s["qk_rstd"], l + 1)
                    stt(qk[:, 0:4 * T], qk[:, 0:4 * T], pr("qw"), qk_rs[:, 0:4 * T], ALU.mult,
                        ALU.mult).then_inc(s["qk_norm"], 1)
                    stt(qk[:, 4 * T:], qk[:, 4 * T:], pr("kw"), qk_rs[:, 4 * T:], ALU.mult,
                        ALU.mult).then_inc(s["qk_norm"], 1)
                if u == 9:
                    dve.wait_ge(s["qk_rot"], 2 * l + 1)
                    tt(sin_t[:, 0:4 * T].rearrange("p (j t) -> p j t", j=4), pm[:, :, 0:T], bc(c("sin"), 4),
                       ALU.mult).then_inc(s["rot_read"], 1)
                if u == 10:
                    dve.wait_ge(s["qk_rot"], 2 * l + 2)
                    tt(sin_t[:, 4 * T:], PM[0][:, 0:T], c("sin"), ALU.mult).then_inc(s["rot_read"], 1)
                    dve.wait_ge(s["rot_read"], 2 * l + 2)
                    dve.wait_ge(s["qk_cos"], l + 1)
                    tt(qk, qk_rs, sin_t, ALU.add).then_inc(s["qk_rope"], 1)
                for g in {12: (0, 1), 13: (2, 3), 14: (4, 5)}.get(u, ()):
                    dve.wait_ge(s["score"], 7 * l + (g + 1))
                    hs = GRP if g < 2 else 2
                    mask = bc(c("mask_prev")[:, P:] if g < 2 else c("mask_prev"), hs)
                    pv = prob[:, g].rearrange("p (a n) -> p a n", a=hs)
                    stt(pv, PM[g % 4].rearrange("p (a n) -> p a n", a=hs), HD ** -0.5, mask, ALU.mult,
                        ALU.add).then_inc(s["score_read"], 1)
                    dve.wait_ge(s["score_read"], 7 * l + (g + 1))
                    o = g * 4 if g < 2 else 8 + 2 * (g - 2)
                    last = nc.vector.reduce_max(mx[:, o:o + hs], pv, AX_X)
                    last.then_inc(s["score_max"], 1)
                if u == 15:
                    dve.wait_ge(s["score"], 7 * l + 7)
                    stt(p_samp, PM[2][:, 0:2 * SK].rearrange("p (g n) -> p g n", g=2), HD ** -0.5,
                        c("mask_samp").rearrange("p (g n) -> p g n", g=2), ALU.mult,
                        ALU.add).then_inc(s["score_read"], 1)
                    dve.wait_ge(s["score_read"], 7 * l + 7)
                    nc.vector.reduce_max(mx[:, 16:18], p_samp, AX_X).then_inc(s["score_max"], 1)
                    dve.wait_ge(s["score_max"], 7 * l + 7)
                    sink2 = bc(pr("sink", 0, 8), 2)
                    v16 = lambda a: a[:, 0:16].rearrange("p (n h) -> p n h", n=2)
                    chain(tt(v16(mx), v16(mx), sink2, ALU.max))
                    chain(ts_(mx[:, 16:18], mx[:, 16:18], pr("sink_s"), None, ALU.max))
                    chain(ts_(negm, mx, -1.0, None, ALU.mult))
                    chain(tt(v16(se), v16(negm), sink2, ALU.add))
                    ts_(se[:, 16:18], negm[:, 16:18], pr("sink_s"), None, ALU.add).then_inc(s["negm"], 1)
                if u == 18:
                    dve.wait_ge(s["prob_e"], 18 * (l + 1))
                    dve.wait_ge(s["sink_e"], l + 1)
                    chain(tt(den, sm, es_, ALU.add))
                    nc.vector.reciprocal(rec, den).then_inc(s["rec"], 1)
                if u == 25:
                    for n in range(2):
                        dve.wait_ge(s["ob_hi"], 4 * l + (n + 1))
                        tt(h_lo[:, 4:8, n * P:(n + 1) * P], PM[3 - 3 * n].rearrange("p (j t) -> p j t", j=4),
                           f(h_hi[:, 4:8, n * P:(n + 1) * P]), ALU.subtract).then_inc(s["ob_lo"], 1)
                    for kv in range(KV):
                        dve.wait_ge(s["ob_hi"], 4 * l + (kv + 3))
                        o, z = samp_out(h_lo, kv)
                        tt(o, z, f(samp_out(h_hi, kv)[0]), ALU.subtract).then_inc(s["ob_lo"], 1)

            def pooling(l, u):
                if u == 16:
                    dve.wait_ge(s["wsum"], l + 1)
                    for g, w in enumerate(WINDOWS):
                        stt(pool_d[:, g, PAD:NP], wsum[g][:, 2 * PAD:PAD + NP], 1.0 / w, uext[:, g, 2 * PAD:PAD + NP],
                            ALU.mult, ALU.subtract).then_inc(s["pool_d"], 1)
                        v = lambda a: a[:, PAD + NP:].rearrange("p (b n) -> p b n", n=SEG)[:, :, PAD:]
                        stt(samp(pool_d[:, g, NP:T]), v(wsum[g]), 1.0 / w, v(uext[:, g]), ALU.mult,
                            ALU.subtract).then_inc(s["pool_d"], 1)
                if u == 18:
                    for g in range(G4):
                        dve.wait_ge(s["oc_hi"], G4 * l + (g + 1))
                        stt(h_lo[:, g], PM[g][:, 0:T], pr("pscale", g), f(h_hi[:, g]), ALU.mult,
                            ALU.subtract).then_inc(s["oc_lo"], 1)

            def hgrn(l, u):
                if u == 26:
                    dve.wait_ge(s["kv_out"], 32 * (l + 1))
                    dve.wait_ge(s["z_read_act"], l * ACT_READS + (U_HG + 4))
                    stt(X0, ZF, -1.0, ZF, ALU.mult, ALU.max).then_inc(s["hz_abs"], 1)
                if u == 27:
                    dve.wait_ge(s["sig"], 3 * l + 2)
                    tt(ZQ, ZQ, D0, ALU.mult).then_inc(s["hz_q"], 1)
                    for h in range(H):
                        last = ts_(hv(KK)[:, h], hv(KK)[:, h], pr("om", h), None, ALU.mult)
                    last.then_inc(s["hz_k"], 1)
                if u == 28:
                    dve.wait_ge(s["hz_ln1"], l + 1)
                    chain(stt(X1, ZF, 0.0, X0, ALU.min, ALU.subtract))
                    for h in range(H):
                        last = ts_(hv(X0)[:, h], hv(X1)[:, h], pr("log_om", h), pr("log_lb", h), ALU.add, ALU.max)
                    chain(last)
                    for h in range(H):
                        last = ts_(hv(X1)[:, h], hv(X1)[:, h], pr("log_om", h), pr("log_lb", h), ALU.add, ALU.min)
                    chain(last)
                    dve.wait_ge(s["hz_q"], l + 1)
                    tt(D0, X1, X0, ALU.subtract).then_inc(s["hz_dif"], 1)
                if u == 29:
                    dve.wait_ge(s["hz_ln2"], l + 1)
                    chain(tt(ZF, X0, D0, ALU.add))
                    for h in range(H):
                        last = nc.vector.tensor_tensor_scan(hv(GG)[:, h], c("seg"), hv(ZF)[:, h], 0.0, ALU.mult,
                                                            ALU.add)
                    chain(last)
                    dve.wait_ge(s["silu_g"], l + 1)
                    g2 = hv(GG)[:, :, 0:NP].rearrange("p h (n t) -> p h n t", n=NB)
                    d2 = D1[:, :, 0:NP].rearrange("p h (n t) -> p h n t", n=NB)
                    tt(d2, g2[:, :, :, P - 1:P].to_broadcast([P, H, NB, P]), g2,
                       ALU.subtract).then_inc(s["end_g"], 1)
                    g3 = hv(GG)[:, :, NP:T].rearrange("p h (b t) -> p h b t", t=TS)
                    d3 = D1[:, :, NP:T].rearrange("p h (b t) -> p h b t", t=TS)
                    tt(d3, g3[:, :, :, TS - 1:TS].to_broadcast([P, H, B, TS]), g3,
                       ALU.subtract).then_inc(s["end_g"], 1)
                if u == 31:
                    dve.wait_ge(s["E0"], l + 1)
                    tt(ZF, ZQ, X0, ALU.mult).then_inc(s["QE"], 1)
                    nc.vector.tensor_copy(ep, hv(X0)[:, :, NP - 1:NP].rearrange("p h o -> p (h o)"))
                    nc.vector.tensor_copy(es.rearrange("p (b h) -> p h b", b=B),
                                          hv(X0)[:, :, NP + TS - 1:T:TS]).then_inc(s["ends"], 1)
                    dve.wait_ge(s["E1"], l + 1)
                    dve.wait_ge(s["hz_k"], l + 1)
                    tt(hv(X1), hv(KK), D1[:], ALU.mult).then_inc(s["KE"], 1)
                if u == 35:
                    dve.wait_ge(s["sfin"], l + 1)
                    dve.wait_ge(s["ends"], l + 1)
                    dve.wait_ge(s["i_tr"], l + 1)
                    for h in range(H):
                        last = ts_(ZI[:, h * P:(h + 1) * P], PM[0][:, h * P:(h + 1) * P], ep[:, h:h + 1], None,
                                   ALU.mult)
                    chain(last)
                    tt(ZI[:, 0:512], ZI[:, 0:512], PM[1], ALU.add).then_inc(s["sfin_read"], 1)
                    dve.wait_ge(s["at_zero"], 2 * l + 2)
                    keep(l, 1, len(LEVELS), 2)
                if 34 <= u <= 46 and u % 2 == 0:
                    i = (u - 34) // 2
                    m = LEVELS[i]
                    D = (D0, D1[:].rearrange("p h t -> p (h t)"))[i % 2]
                    if i >= 2:
                        dve.wait_ge(s["level_x"], 14 * l + 2 * (i - 1))
                    g0, g1 = level_views(GG, m)
                    d0, d1 = level_views(D, m)
                    ref = g0[:, :, :, m - 1:m].to_broadcast(list(g0.shape))
                    tt(d0, ref, g0, ALU.subtract).then_inc(s["level_d"], 1)
                    tt(d1, g1, ref, ALU.subtract).then_inc(s["level_d"], 1)
                if 35 <= u <= 47 and u % 2:
                    i = (u - 35) // 2
                    m = LEVELS[i]
                    D = (D0, D1[:].rearrange("p h t -> p (h t)"))[i % 2]
                    X = (X0, X1)[i % 2]
                    dve.wait_ge(s["level_e"], 7 * l + (i + 1))
                    if i == 0:
                        dve.wait_ge(s["cross"], l + 1)
                        dve.wait_ge(s["ends"], l + 1)
                    if i == 1:
                        dve.wait_ge(s["cross"], l + 1)
                    if i >= 2:
                        dve.wait_ge(s["level_mm"], 11 * l + (i + 1))
                    d0, d1 = level_views(D, m)
                    x0, x1 = level_views(X, m)
                    tt(x0, level_views(KK, m)[0], d0, ALU.mult).then_inc(s["level_x"], 1)
                    tt(x1, level_views(ZQ, m)[1], d1, ALU.mult).then_inc(s["level_x"], 1)
                if u == 37:
                    keep_sample(l, 2, len(LEVELS), 2)
                if 37 <= u <= 49 and u % 2:
                    i = (u - 37) // 2
                    keep(l, (3 + i) if i < 6 else 10, i, 2 * (i % 2))
                    if i == 5:
                        keep_sample(l, 9, 5, 0)
                    if i == 6:
                        keep_sample(l, 11, 6, 2)
                if u == 54:
                    dve.wait_ge(s["o_rstd"], l + 1)
                    dve.wait_ge(s["o_sb"], 3 * l + 3)
                    chain(stt(X0, ZI, pr("onorm"), D1[:].rearrange("p h t -> p (h t)"), ALU.mult, ALU.mult))
                    tt(X0, X0, ZG, ALU.mult).then_inc(s["oa"], 1)
                if u == 55:
                    dve.wait_ge(s["oa_hi"], l + 1)
                    tt(a_lo[:, 0:4], hv(X0), f(a_hi[:, 0:4]), ALU.subtract).then_inc(s["oa_lo"], 1)
                if u in (58, 60):
                    for h in ((0, 1) if u == 58 else (2, 3)):
                        dve.wait_ge(s["snew"], 4 * l + (h + 1))
                        dve.wait_ge(s["s0_decay"], l + 1)
                        b0 = 2 * (h % 2)
                        tt(S0v[:, :, h], S0v[:, :, h],
                           pm[:, b0:b0 + 2].rearrange("p c (b n) -> p (c b) n", n=P), ALU.add).then_inc(s["snew_read"], 1)

            def keep(l, product, level, bank):
                dve.wait_ge(s["level_mm"], 11 * l + product)
                dve.sem_inc(s["dve_passed"], 1)
                dve.wait_ge(s["lmask_ready"], 1)
                m = lmask[:, level]
                for n in range(NB):
                    last = nc.vector.copy_predicated(AT[:, n], bc(m, H), PM[bank + n].rearrange("p (h t) -> p h t", h=H))
                last.then_inc(s["level_read"], 1)

            def keep_sample(l, product, level, bank):
                dve.wait_ge(s["level_mm"], 11 * l + product)
                dve.sem_inc(s["dve_passed"], 1)
                dve.wait_ge(s["lmask_ready"], 1)
                last = nc.vector.copy_predicated(ATsv[0:NS], bc(lmask[0:NS, level, 0:NS], H),
                                                 PM[bank][0:NS, 0:H * NS].rearrange("p (h t) -> p h t", h=H))
                last.then_inc(s["level_read"], 1)

            def branches(l, u):
                n, half = 2 - (u - U_BR) // 4, (u - U_BR) % 4
                for k in range(2):
                    d = 2 * half + k
                    t = T_BR + 2 * (u - U_BR) + k
                    if k == 0:
                        dve.wait_ge(s["half_done"], 12 * l + (u - U_BR + 1))
                    else:
                        dve.wait_ge(s["unit_done"], l * UNITS + (u + 1) + HEAD)
                    dve.wait_ge(s["gate"], 3 * l + (3 - n))
                    tt(gates[:, n, d], gates[:, n, d], PZ[t % 4][:, 0:T], ALU.mult).then_inc(s["z_read_dve"], 1)
                    if n == 0:
                        dve.wait_ge(s["z_read_dve"], l * DVE_READS + (t - T_BR + 1) + HEAD)
                        dve.wait_ge(s["acc"], l * KT + (d + 1))
                        tt(gates[:, 2, d], gates[:, 2, d], gates[:, 0, d], ALU.add).then_inc(s["merged"], 1)

            def merged_lo(l, ds_):
                for d in ds_:
                    dve.wait_ge(s["m_hi"], l * KT + (d + 1))
                    tt(h_lo[:, d], gates[:, 2, d], f(h_hi[:, d]), ALU.subtract).then_inc(s["m_lo"], 1)

            def mlp(l, i, last):
                for j in range(16):
                    if j < 8:
                        dve.wait_ge(s["z_read_act"], l * ACT_READS + i * 8 + (T_BR + j + 1))
                        dve.wait_ge(s["f_lo"], l * 8 * FI + i * 8 + max(j - 1, 0) + HEAD)
                        tt(hsq[:, j % 2], relu[:, j % 2], relu[:, j % 2], ALU.mult).then_inc(s["hsq"], 1)
                    if 1 <= j < 9:
                        dve.wait_ge(s["f_hi"], l * 8 * FI + i * 8 + j)
                        tt(h_lo[:, j - 1], hsq[:, (j - 1) % 2], f(h_hi[:, j - 1]),
                           ALU.subtract).then_inc(s["f_lo"], 1)
                    if j >= 8:
                        add_to_x(l, j - 8, PZ[(T_FFN + j) % 4], l * UNITS + i * 16 + (U_FFN + j + 1))
                    if j + LEAD < 16 or not last:
                        split(l, U_FFN + j + LEAD, i)
                    if last and j > 8:
                        add_square(2 * l + 3, j - 9)
                if last:
                    add_square(2 * l + 3, 7)

            for name in ("w_lo", "z_read_dve", "ssum", "hsq", "f_lo", "oa_lo", "snew_read"):
                dve.sem_inc(s[name], HEAD)
            dve.wait_ge(s["params_landed"], 16)
            lbs = params[:, :, PAR["lb"][0]:PAR["lb"][0] + H]
            e = small[:, 0:2 * H].rearrange("p (l h) -> p l h", l=DEPTH)
            prep = Chain(dve, "prep_chain", 0)
            t = lambda k: small[:, 16 + 4 * k:20 + 4 * k]
            prep(tt(t(0), lbs[:, 0], lbs[:, 1], ALU.max))
            for k in range(DEPTH):
                last = tt(e[:, k], lbs[:, k], t(0), ALU.subtract)
            last.then_inc(s["prep_v"], 1)
            dve.wait_ge(s["prep_a"], 1)
            prep(tt(t(1), e[:, 0], e[:, 1], ALU.add))
            prep(nc.vector.reciprocal(t(2), t(1)))
            for k in range(DEPTH):
                prep(tt(e[:, k], e[:, k], t(2), ALU.mult))
            tiny = 2.0 ** -60
            for k in range(DEPTH):
                if k == 0:
                    prep(nc.vector.tensor_copy(t(0), e[:, 0]))
                else:
                    prep(tt(t(0), t(0), e[:, k], ALU.add))
                prep(tt(t(3), t(0), e[:, 0], ALU.subtract))
                prep(ts_(t(3), t(3), 0.0, None, ALU.max))
                om = params[:, k, PAR["om"][0]:PAR["om"][0] + H]
                prep(ts_(om, t(3), -1.0, 1.0, ALU.mult, ALU.add))
                o = 32 + 12 * k
                prep(ts_(small[:, o:o + H], om, tiny, None, ALU.max))
                prep(ts_(small[:, o + H:o + 2 * H], t(3), LB_FLOOR, tiny, ALU.max, ALU.max))
                prep(ts_(t(3), t(3), LB_FLOOR, 1.0 / tiny, ALU.max, ALU.mult))
                last = ts_(small[:, o + 2 * H:o + 3 * H], t(3), 1.0, None, ALU.min)
                if k < DEPTH - 1:
                    prep(last)
            last.then_inc(s["prep_v"], 1)
            dve.wait_ge(s["prep_a"], 2)
            for k in range(DEPTH):
                o = 32 + 12 * k
                prep(nc.vector.tensor_copy(params[:, k, PAR["log_om"][0]:PAR["log_om"][0] + H], small[:, o:o + H]))
                prep(tt(params[:, k, PAR["log_lb"][0]:PAR["log_lb"][0] + H], small[:, o + H:o + 2 * H],
                        small[:, o + 2 * H:o + 3 * H], ALU.add))
            dve.wait_ge(s["x_landed"], 16)
            dve.wait_ge(s["consts_landed"], 16)
            for j in range(KT):
                add_square(1, j)
            with dve.Fori(0, DEPTH) as l:
                chain.layer(l * DVE_CHAIN)
                chain(nc.vector.tensor_copy(par[:], params[:, bass.ds(l, 1), :].rearrange("p o n -> p (o n)")))
                split(l, 0)
                split(l, 1)
                norm(2 * l + 1, "norm_mix")
                for u in range(U_FFN):
                    if U_BR <= u < U_O:
                        branches(l, u)
                    if u >= U_O:
                        add_to_x(l, u - U_O, PZ[(T_O + u - U_O) % 4], l * UNITS + (u + 1))
                        if u > U_O:
                            add_square(2 * l + 2, u - U_O - 1)
                    split(l, u + LEAD)
                    if U_BR + 8 <= u < U_O:
                        merged_lo(l, (2 * (u - U_BR - 8), 2 * (u - U_BR - 8) + 1))
                    attention(l, u)
                    pooling(l, u)
                    hgrn(l, u)
                add_square(2 * l + 2, 7)
                norm(2 * l + 2, "norm_ffn")
                with dve.Fori(0, FI - 1) as i:
                    mlp(l, i, False)
                mlp(l, FI - 1, True)
                assert chain.k == DVE_CHAIN, chain.k

        @block.gpsimd
        def _(pool):
            chain = Chain(pool, "pool_chain", 0)
            pool.wait_ge(s["lmask_landed"], 16)
            nc.gpsimd.tensor_copy(lmask[:].rearrange("p l t -> p (l t)"),
                                  A[:, 8 * P * 4:8 * P * 5]).then_inc(s["lmask_ready"], 1)
            tt = nc.gpsimd.tensor_tensor
            pool.sem_inc(s["s0_free"], HEAD)
            pool.dma_start(io["kc_out"], io["kc_kept"]).then_inc(s["cache_out"], 16)
            pool.dma_start(io["vc_out"], io["vc_kept"]).then_inc(s["cache_out"], 16)
            pool.wait_ge(s["consts_landed"], 16)
            with pool.Fori(0, DEPTH) as l:
                chain.layer(l * POOL_CHAIN)
                pool.wait_ge(s["qk_norm"], 2 * l + 2)
                q5 = qk.rearrange("p (j t) -> p j t", t=T)
                tt(qk_rs.rearrange("p (j t) -> p j t", t=T), q5, bc(c("cos"), 5), ALU.mult).then_inc(s["qk_cos"], 1)
                nc.gpsimd.memset(uext[:, :, 0:PAD], 0.0).then_inc(s["u_front"], 1)
                chain(nc.gpsimd.memset(q_samp, 0.0))
                pool.wait_ge(s["qk_rope"], l + 1)
                pool.wait_ge(s["u_front"], l + 1)
                pool.sem_inc(s["pool_passed"], 1)
                for kv in range(KV):
                    if kv:
                        pool.wait_ge(s["q_samp"], 2 * l + kv)
                        pool.sem_inc(s["pool_passed"], 1)
                    rows = slice(kv * HD, (kv + 1) * HD)
                    o = q_samp.rearrange("p (b k j t) -> p b k j t", b=B, k=KV, j=GRP)[rows, :, kv]
                    i_ = q5[rows, 0:4, NP:T].rearrange("p j (b t) -> p b j t", t=TS)
                    nc.gpsimd.tensor_copy(o, i_).then_inc(s["q_samp"], 1)
                pool.wait_ge(s["q_samp"], 2 * l + 2)
                pool.dma_start(io["k_out"][l], qk[:, 4 * T:]).then_inc(s["kv_out"], 16)
                pool.dma_start(io["v_out"][l], vz).then_inc(s["kv_out"], 16)
                pool.wait_ge(s["z_read_act"], l * ACT_READS + (U_U + 4))
                pool.wait_ge(s["ustate_landed"], 16 * (l + 1))
                pool.wait_ge(s["u_front"], l + 1)
                pool.dma_start(io["u_out"][l], S0[:, 0:G4 * UX]).then_inc(s["u_out"], 16)
                chain(tt(wa[:, :, 1:], uext[:, :, 1:], uext[:, :, :-1], ALU.add))
                chain(tt(wb[:, :, 3:], wa[:, 1:4, 3:], wa[:, 1:4, 1:-2], ALU.add))
                chain(tt(wa[:, 2:4, 7:], wb[:, 1:3, 7:], wb[:, 1:3, 3:-4], ALU.add))
                chain(tt(wb[:, 2, 15:], wa[:, 3, 15:], wa[:, 3, 7:-8], ALU.add))
                for g in range(G4):
                    last = tt(first[:, g], wsum[g][:, PAD:2 * PAD],
                              c("invcnt").rearrange("p (g n) -> p g n", g=G4)[:, g], ALU.mult)
                last.then_inc(s["wsum"], 1)
                last = None
                pool.wait_ge(s["wsum"], l + 1)
                tt(pool_d[:, :, 0:PAD], first, uext[:, :, PAD:2 * PAD], ALU.subtract).then_inc(s["pool_first"], 2)
                pool.wait_ge(s["rec"], l + 1)
                for g in range(7):
                    if g < 6:
                        hs, o = (GRP, g * 4) if g < 2 else (2, 8 + 2 * (g - 2))
                        a = prob[:, g].rearrange("p (a n) -> p a n", a=hs)
                    else:
                        hs, o, a = 2, 16, p_samp
                    tt(a, a, bl(rec[:, o:o + hs], a.shape[2]), ALU.mult).then_inc(s["prob_n"], 1)
                pool.wait_ge(s["sig"], 3 * l + 3)
                tt(hv(ZG), hv(ZG), D1[:], ALU.mult).then_inc(s["silu_g"], 1)
                pool.wait_ge(s["sfin"], l + 1)
                pool.sem_inc(s["pool_passed"], 1)
                nc.gpsimd.memset(AT[:], 0.0).then_inc(s["at_zero"], 1)
                nc.gpsimd.memset(ATs, 0.0).then_inc(s["at_zero"], 1)
                pool.wait_ge(s["sfin_read"], l + 1)
                pool.dma_start(io["sp_out"][l].rearrange("p h n -> p (h n)"), ZI[:, 0:512]).then_inc(s["sp_out"], 16)
                pool.wait_ge(s["o_ps"], 3 * l + 3)
                for h in range(H):
                    im = (KK, GG, X1, ZF)[h][0:NS, 0:B * P].rearrange("p (b n) -> p b n", b=B)
                    tt(im, bc(itok[0:NS, 2, h], B), bl(c("bmask", slice(0, NS)), P), ALU.mult).then_inc(s["imask"], 1)
                tt(S0.rearrange("p (b n) -> p b n", n=P), S0.rearrange("p (b n) -> p b n", n=P), bl(es, P),
                   ALU.mult).then_inc(s["s0_decay"], 1)
                for d in range(KT):
                    pool.wait_ge(s["z_read_dve"], l * DVE_READS + (8 + d + 1) + HEAD)
                    tt(gates[:, 2, d], gates[:, 2, d], gates[:, 1, d], ALU.add).then_inc(s["acc"], 1)
                pool.wait_ge(s["snew_read"], 4 * l + 4 + HEAD)
                pool.dma_start(io["ss_out"][l].rearrange("p b n -> p (b n)"), S0).then_inc(s["ss_out"], 16)
                pool.wait_ge(s["ss_out"], 16 * (l + 1))
                pool.sem_inc(s["s0_free"], 1)
                assert chain.k == POOL_CHAIN, chain.k
            for name, n in (("cache_out", 32), ("kv_out", 32 * DEPTH), ("u_out", 16 * DEPTH),
                            ("sp_out", 16 * DEPTH), ("ss_out", 16 * DEPTH)):
                pool.wait_ge(s[name], n)


DVE_CHAIN = 13
POOL_CHAIN = 5


def _weights(w_in, w_branch, w_o, w_up, w_down):
    out = np.empty((DEPTH, UNITS, P, UW), w_in.dtype)

    def tiles(w):
        k, n = w.shape
        return w.reshape(k // P, P, n // P, P).transpose(2, 1, 0, 3)

    for l in range(DEPTH):
        w = w_in[l]
        q = w[:, 0:512].reshape(D_MODEL, KV, GRP, HD).transpose(0, 2, 1, 3).reshape(D_MODEL, 512)
        kv, hq, hf, hi, hg, u = (w[:, a:b] for a, b in (
            (512, 768), (768, 1280), (1280, 1792), (1792, 2304), (2304, 2816), (2816, 3328)))
        z = [w[:, 3328 + n * D_MODEL:3328 + (n + 1) * D_MODEL] for n in (2, 1, 0)]
        a = np.concatenate([q, kv, u, hf, hq, hi, hg] + z, 1)
        out[l, 0:U_BR] = tiles(a).reshape(U_BR, P, UW)
        for i, n in enumerate((2, 1, 0)):
            wb = w_branch[l, n]
            if n == 1:
                wb = wb.reshape(KV, GRP, HD, D_MODEL).transpose(1, 0, 2, 3).reshape(512, D_MODEL)
            out[l, U_BR + 4 * i:U_BR + 4 * i + 4] = (
                wb.reshape(4, P, 4, 256).transpose(2, 1, 0, 3).reshape(4, P, UW))
        out[l, U_O:U_FFN] = tiles(w_o[l]).reshape(8, P, UW)
        up = tiles(w_up[l]).reshape(FI, 8, P, UW)
        down = w_down[l].reshape(FI, KT, P, KT, P).transpose(0, 3, 2, 1, 4).reshape(FI, 8, P, UW)
        out[l, U_FFN:] = np.concatenate([up, down], 1).reshape(FI * 16, P, UW)
    return out


def _params(d):
    def col(a):
        return np.asarray(a).reshape(-1, P).T

    rows = []
    for l in range(DEPTH):
        sink = np.asarray(d["attn_sinks"][l])
        rows.append(np.concatenate([
            col(d["norm_mix"][l]), col(d["norm_ffn"][l]),
            np.tile(d["q_norm"][l], 2)[:, None], np.tile(d["k_norm"][l], 2)[:, None],
            np.tile(sink[None], (P, 1)), np.tile(np.repeat(sink, TS), 4)[:, None],
            np.asarray(d["hgrn_onorm"][l])[:, None], col(d["pool_scale"][l]), col(d["hgrn_lb"][l])], 1))
    return np.ascontiguousarray(np.stack(rows, 1))


def kernel(**inputs):
    import concourse.bacc as _bacc
    from concourse.bass_utils import run_bass_kernel_spmd as _run

    d = {k: np.asarray(v) for k, v in inputs.items()}
    con = _constants()
    xs = d["x_sample"].reshape(NS, D_MODEL)
    xt = np.concatenate([d["x_prompt"].reshape(NP, D_MODEL), xs], 0)
    kc, vcache = (d[k].reshape(DEPTH, B, P, P) for k in ("cache_swa_k", "cache_swa_v"))
    state = np.zeros((DEPTH, P, G4, B, SEG), d["state_pool"].dtype)
    state[..., 1:PAD] = d["state_pool"].reshape(DEPTH, B, PAD - 1, G4, P).transpose(0, 4, 3, 1, 2)
    arrays = {
        "x_in": xt.reshape(T, KT, P).transpose(2, 1, 0),
        "w": _weights(d["w_in"], d["w_branch"], d["w_o"], d["w_up"], d["w_down"]),
        "params": _params(d),
        "consts": con,
        "lmask": _level_masks(),
        "kcT": kc.transpose(0, 3, 1, 2),
        "vc": vcache.transpose(0, 2, 1, 3),
        "pool_w": d["pool_w"].transpose(0, 2, 1, 3),
        "pool_state": state.reshape(DEPTH, P, G4, B * SEG),
        "s0": d["state_hgrn"].transpose(0, 3, 1, 2, 4).reshape(DEPTH, P, B * H * P),
        "kc_kept": kc[:, :, TS:].reshape(DEPTH * B, (P - TS) * P),
        "vc_kept": vcache[:, :, TS:].reshape(DEPTH * B, (P - TS) * P),
    }
    nc = _bacc.Bacc("TRN2", target_bir_lowering=False, num_devices=1)
    io, sent = {}, {}
    for name, a in arrays.items():
        a = np.ascontiguousarray(a)
        sent[f"in_{name}"] = a
        io[name] = nc.dram_tensor(f"in_{name}", a.shape, mybir.dt.from_np(a.dtype), kind="ExternalInput").ap()
    for name, shape in OUT_SHAPES.items():
        io[name] = nc.dram_tensor(f"out_{name}", shape, F32, kind="ExternalOutput").ap()
    build(nc, io)
    r = _run(nc, [sent], core_ids=[0]).results[0]
    got = {name: r[f"out_{name}"] for name in OUT_SHAPES}

    y = got["y"].transpose(2, 1, 0).reshape(T, D_MODEL)
    ko, vo = got["k_out"], got["v_out"]
    heads = (KV, HD)

    def cache(kept, new):
        k = kept.reshape(DEPTH, B, P - TS, P)
        n = new[:, :, NP:].reshape(DEPTH, P, B, TS).transpose(0, 2, 3, 1)
        return np.concatenate([k, n], 2).reshape(DEPTH, B, P, *heads)

    def prompt_cache(a):
        return np.ascontiguousarray(a[:, :, NP - P:NP].transpose(0, 2, 1)).reshape(DEPTH, 1, P, *heads)

    u = got["u_out"].reshape(DEPTH, P, G4, UX)
    pool_p = u[..., PAD + NP - 15:PAD + NP].transpose(0, 3, 2, 1).reshape(DEPTH, 1, 15, G4 * P)
    pool_s = u[..., PAD + NP:].reshape(DEPTH, P, G4, B, SEG)[..., SEG - 15:]
    pool_s = pool_s.transpose(0, 3, 4, 2, 1).reshape(DEPTH, B, 15, G4 * P)
    sp_ = got["sp_out"].transpose(0, 2, 1, 3).reshape(DEPTH, 1, H, P, P)
    ss_ = got["ss_out"].reshape(DEPTH, P, B, H, P).transpose(0, 2, 3, 1, 4)
    c_ = np.ascontiguousarray
    return (c_(y[:NP]).reshape(1, NP, D_MODEL), c_(y[NP:]).reshape(B, TS, D_MODEL),
            c_(sp_), prompt_cache(ko), prompt_cache(vo), c_(pool_p),
            c_(ss_), cache(got["kc_out"], ko), cache(got["vc_out"], vo), c_(pool_s))
```

```python
from contextlib import ExitStack

import numpy as np

import concourse.bass as bass
from concourse import mybir

F32 = mybir.dt.float32
F32R = mybir.dt.float32r
U8 = mybir.dt.uint8
ACT = mybir.ActivationFunctionType
ALU = mybir.AluOpType
AX_X = mybir.AxisListType.X

P = 128
DEPTH = 2
D_MODEL = 1024
KT = D_MODEL // P
NP = 256
B = 8
TS = 4
NS = B * TS
T = NP + NS
HD = 64
KV = 2
GRP = 4
H = 4
NB = NP // P
G4 = 4
WINDOWS = (2, 4, 8, 16)
PAD = 16
SEG = PAD + TS
UX = PAD + NP + B * SEG
SK = P + NS
EPS = 1e-6
NEG = -1e30
LB_FLOOR = 1e-30
LEVELS = (64, 32, 16, 8, 4, 2, 1)
HEAD = 1

U_Q, U_K, U_V, U_U, U_HF, U_HQ, U_HI, U_HG = 0, 4, 5, 6, 10, 14, 18, 22
U_GATE = 26
U_BR = 50
U_O = 62
U_FFN = 70
FI = 4
UNITS = U_FFN + FI * 16
RING = 4
LEAD = 3
UW = 1024
PER_SLOT = [len(range(r, UNITS, RING)) for r in range(RING)]
T_BR, T_O, T_FFN = 50, 74, 82
ACT_READS = T_BR - U_GATE
DVE_READS = U_GATE + (T_FFN - T_BR) + 16 * FI

C = {}


def _constants():
    cols = []
    at = 0

    def put(name, a):
        nonlocal at
        a = np.asarray(a, np.float32).reshape(P, -1)
        C[name] = (at, a.shape[1])
        at += a.shape[1]
        cols.append(a)

    p = np.arange(P)
    put("ident", np.eye(P))
    put("ones", np.ones((P, P)))
    put("headones", (p[:, None] // HD == p[None, :] // HD))
    perm = np.zeros((P, P))
    for i in range(P):
        if i % HD < HD // 2:
            perm[i + HD // 2, i] = -1.0
        else:
            perm[i - HD // 2, i] = 1.0
    put("perm", perm)
    pos = np.concatenate([np.arange(NP), np.tile(1024 + np.arange(TS), B)]).astype(np.float32)
    inv = np.power(np.float32(10000.0), -np.arange(0, HD, 2, dtype=np.float32) / HD).astype(np.float32)
    ang = (pos[None, :] * inv[p % (HD // 2)][:, None]).astype(np.float32)
    q, k = p[:, None], p[None, :]
    put("mask_prev", np.concatenate([np.where(k > q, 0.0, NEG), np.where(k <= q, 0.0, NEG)], 1))
    t_row, b_row = p % TS, p // 32
    ms = []
    for g in range(2):
        j = np.arange(P)[None, :]
        cache = np.where(j > t_row[:, None], 0.0, NEG)
        n = np.arange(NS)[None, :]
        new = np.where((n // TS == (4 * g + b_row)[:, None]) & (n % TS <= t_row[:, None]), 0.0, NEG)
        ms.append(np.concatenate([cache, new], 1))
    put("mask_samp", np.stack(ms, 1))
    e = np.arange(PAD)
    put("invcnt", np.tile(np.stack([1.0 / np.minimum(w, e + 1) for w in WINDOWS])[None], (P, 1, 1)))
    seg = np.ones(T)
    seg[[0, P]] = 0.0
    seg[NP::TS] = 0.0
    put("seg", np.tile(seg[None], (P, 1)))
    put("bmask", (p[:, None] // TS == np.arange(B)[None, :]))
    put("eps", np.full((P, 1), EPS))
    put("one", np.ones((P, 1)))
    return np.ascontiguousarray(np.concatenate(cols, 1)), np.concatenate([np.cos(ang), np.sin(ang)], 1)


def _level_masks():
    s, t = np.arange(P)[:, None], np.arange(P)[None, :]
    ms = [(s // (2 * m) == t // (2 * m)) & (s % (2 * m) < m) & (t % (2 * m) >= m) for m in LEVELS]
    ms.append(s == t)
    return np.ascontiguousarray(np.stack(ms, 1).astype(np.float32)).reshape(P, -1)


PAR = {}
_at = 0
for _name, _n in (("norm_next", KT), ("norm_ffn", KT), ("qw", 1), ("kw", 1), ("sink", 8), ("sink_s", 1),
                  ("onorm", 1), ("pscale", G4), ("lb", H)):
    PAR[_name] = (_at, _n)
    _at += _n
NPAR_IN = _at
for _name in ("log_lb", "log_om", "om"):
    PAR[_name] = (_at, H)
    _at += H
NPAR = _at

OUT_SHAPES = {
    "y": (P, KT, T), "k_out": (DEPTH, P, T), "v_out": (DEPTH, P, T), "u_out": (DEPTH, P, G4 * UX),
    "sp_out": (DEPTH, P, H, P), "ss_out": (DEPTH, P, B * H, P),
    "kc_out": (DEPTH * B, (P - TS) * P), "vc_out": (DEPTH * B, (P - TS) * P),
}


def build(nc, io):
    _constants()
    ctx = ExitStack()
    with ctx:
        def sb(name, shape, dt=F32):
            return ctx.enter_context(nc.sbuf_tensor(name, shape, dt))

        raw = sb("raw", [P, RING, UW])
        w_hi = sb("w_hi", [P, RING, UW], F32R)
        w_lo = sb("w_lo", [P, RING, UW], F32R)
        x = sb("x", [P, KT, T])
        a_hi = sb("a_hi", [P, KT, T], F32R)
        a_lo = sb("a_lo", [P, KT, T], F32R)
        h_hi = sb("h_hi", [P, KT, T], F32R)
        h_lo = sb("h_lo", [P, KT, T], F32R)
        consts = sb("consts", [P, sum(n for _, n in C.values())])
        lmask = sb("lmask", [P, len(LEVELS) + 1, P], U8)
        params = sb("params", [P, DEPTH, NPAR])
        par = sb("par", [P, NPAR])
        poolw = sb("poolw", [P, G4, P])
        small = sb("small", [P, 164])
        rstd = sb("rstd", [P, T])
        pool_d = sb("pool_d", [P, G4, T])
        HT = H * T
        sizes = [("A", 3 * KT * T), ("ZF", HT), ("ZQ", HT), ("ZI", HT), ("ZG", HT), ("R", 5 * HT),
                 ("itok", 3 * 512), ("ktok", 2 * 512), ("AC", 512), ("ktok_s", 512), ("ATs", 128),
                 ("S0", B * H * P)]
        arena = sb("arena", [P, sum(n for _, n in sizes)])
        reg, at = {}, 0
        for name, n in sizes:
            reg[name] = arena[:, at:at + n]
            at += n
        A, ZF, ZQ, ZI, ZG, R, ktok, AC, ATs, S0 = (
            reg[n] for n in ("A", "ZF", "ZQ", "ZI", "ZG", "R", "ktok", "AC", "ATs", "S0"))

        def c(name, rows=slice(0, P)):
            o, n = C[name]
            return consts[rows, o:o + n]

        def pr(name, i=0, n=1):
            o = PAR[name][0] + i
            return par[:, o:o + n]

        def bc(a, n):
            return a.rearrange("p (o m) -> p o m", o=1).to_broadcast([a.shape[0], n, a.shape[1]])

        def bl(a, n):
            return a.rearrange("p (m o) -> p m o", o=1).to_broadcast([a.shape[0], a.shape[1], n])

        def hv(a):
            return a.rearrange("p (h t) -> p h t", t=T)

        gates = A.rearrange("p (n k t) -> p n k t", n=3, k=KT)
        sq = A[:, 0:2 * T].rearrange("p (s t) -> p s t", s=2)
        ssum = A[:, 2 * T:3 * T]
        relu = A[:, 12 * T:14 * T].rearrange("p (s t) -> p s t", s=2)
        hsq = A[:, 14 * T:16 * T].rearrange("p (s t) -> p s t", s=2)
        sin_t = A[:, 0:5 * T]
        prob = A[:, 0:3072].rearrange("p (g n) -> p g n", g=6)
        probT = A[:, 3072:6144].rearrange("p (g n) -> p g n", g=6)
        qk = R[:, 0:5 * T]
        qk_rs = R[:, 5 * T:10 * T]
        kcT = R[:, 10 * T:10 * T + B * P].rearrange("p (b s) -> p b s", b=B)
        vc = R[:, 10 * T + B * P:10 * T + 2 * B * P].rearrange("p (b n) -> p b n", b=B)
        tail = R[:, 10 * T + 2 * B * P:5 * HT]
        vz = tail[:, 0:T]
        v_tok = tail[:, T:T + 384].rearrange("p (b n) -> p b n", b=3)
        q_samp = AC[:, 0:256]
        psT = AC[:, 256:512].rearrange("p (g n) -> p g n", g=2)
        p_samp = reg["ktok_s"][:, 0:2 * SK].rearrange("p (g n) -> p g n", g=2)
        pnT = ktok[:, 0:256].rearrange("p (g n) -> p g n", g=2)
        uext = S0[:, 0:G4 * UX].rearrange("p (g n) -> p g n", g=G4)
        wa = S0[:, G4 * UX:2 * G4 * UX].rearrange("p (g n) -> p g n", g=G4)
        first = S0[:, 2 * G4 * UX:2 * G4 * UX + G4 * PAD].rearrange("p (g n) -> p g n", g=G4)
        cos = S0[:, B * H * P - 2 * T:B * H * P - T]
        sin = S0[:, B * H * P - T:B * H * P]
        wb = reg["itok"][:, 0:3 * UX].rearrange("p (g n) -> p g n", g=3)
        wsum = [wa[:, 0], wb[:, 0], wa[:, 2], wb[:, 2]]
        KK, D1, D0, X0, X1 = (R[:, i * HT:(i + 1) * HT] for i in range(5))
        GG = pool_d[:].rearrange("p h t -> p (h t)")
        LF = reg["itok"][:, 0:HT]

        itok = reg["itok"].rearrange("p (b h n) -> p b h n", b=3, h=H)
        ktok4 = ktok.rearrange("p (b h n) -> p b h n", b=NB, h=H)
        ktok_s = reg["ktok_s"].rearrange("p (h n) -> p h n", h=H)
        AT = ktok.rearrange("p (b h t) -> p b h t", b=NB, h=H)
        ACv = AC.rearrange("p (h t) -> p h t", h=H)
        ATsv = ATs.rearrange("p (h t) -> p h t", h=H)
        S0v = S0.rearrange("p (b h n) -> p b h n", b=B, h=H)

        PZ = [ctx.enter_context(nc.psum_tensor(f"pz{i}", [P, 512], F32)) for i in range(4)]
        pm = ctx.enter_context(nc.psum_tensor("pm", [P, 4, 512], F32))
        PM = [pm[:, i, :] for i in range(4)]

        def cols(o, n):
            return small[:, o:o + n]
        mx, negm, sm, se, es_, den, rec = (cols(18 * i, 18) for i in range(7))
        ep, es = cols(126, H), cols(130, B * H)

        made = {}

        class Sems:
            def __getitem__(self, name):
                if name not in made:
                    made[name] = ctx.enter_context(nc.semaphore(name))
                return made[name]
        s = Sems()
        ld = [s[f"raw_landed{r}"] for r in range(RING)]

        class Chain:

            def __init__(self, eng, name, per_layer):
                self.eng, self.sem, self.per_layer, self.base, self.k = eng, s[name], per_layer, 0, 0

            def layer(self, base):
                self.base, self.k = base, 0

            def __call__(self, ins):
                self.k += 1
                ins.then_inc(self.sem, 1)
                self.eng.wait_ge(self.sem, self.base + self.k)

            def close(self):
                assert self.k == self.per_layer, (self.sem, self.k)

        def slot_landed(u, l, i=0):
            return (l * PER_SLOT[u % RING] + (u // RING + 1) + i * (16 // RING)) * 16

        def read_dve(l, t):
            return l * DVE_READS + (t + 1 if t < U_GATE else t + 1 - (T_BR - U_GATE)) + HEAD

        def read_act(l, t):
            return l * ACT_READS + (t + 1 - U_GATE)

        def first_norm(j):
            o = PAR["norm_next"][0] + j
            return params[:, DEPTH - 1, o:o + 1]

        def gate_tile(t):
            return gates[:, 2 - (t - U_GATE) // KT, (t - U_GATE) % KT]

        def level_views(a, m):
            w = T if m <= 2 else NP
            v = hv(a)[:, :, 0:w].rearrange("p h (a e s) -> p h a e s", e=2, s=m)
            return v[:, :, :, 0, :], v[:, :, :, 1, :]

        def samp(a):
            return a.rearrange("p (b t) -> p b t", t=TS)

        def samp_out(h, kv):
            rows = slice(kv * HD, (kv + 1) * HD)
            o = h[rows, 4:8, NP:T].rearrange("p j (b t) -> p b j t", t=TS)
            z = PM[1][rows, 0:256].rearrange("p (b k j t) -> p b k j t", b=B, k=KV, j=GRP)[:, :, kv]
            return o, z

        block = ctx.enter_context(nc.Block())

        @block.sync
        def _(sp):
            def load(l, u, r, used):
                sp.wait_ge(s["w_lo"], used + HEAD)
                sp.dma_start(raw[:, r],
                             io["w"][bass.ds(l * UNITS + u, 1)].rearrange("o p n -> (o p) n")).then_inc(ld[r], 16)

            sp.dma_start(params[:, :, 0:NPAR_IN], io["params"]).then_inc(s["params_landed"], 16)
            for j in range(0, KT, 4):
                if j > 0:
                    load(0, 0, 0, 0)
                sp.dma_start(x[:, j:j + 4], io["x_in"][:, j:j + 4]).then_inc(s[f"x_landed{j}"], 16)
            for u in range(1, RING):
                load(0, u, u, 0)
                if u == 1:
                    sp.dma_start(consts[:], io["consts"]).then_inc(s["consts_landed"], 16)
            with sp.Fori(0, DEPTH) as l:
                sp.wait_ge(s["snew_read"], 4 * l + HEAD)
                sp.sem_inc(s["sp_passed"], 1)
                sp.wait_ge(s["oa_lo"], l + HEAD)
                sp.sem_inc(s["sp_passed"], 1)
                sp.dma_start(kcT, io["kcT"][l]).then_inc(s["cache_landed"], 16)
                sp.dma_start(vc, io["vc"][l]).then_inc(s["cache_landed"], 16)
                sp.wait_ge(s["pool_y"], l + HEAD)
                sp.sem_inc(s["sp_passed"], 1)
                sp.dma_start(poolw[:], io["pool_w"][l]).then_inc(s["poolw_landed"], 16)
                sp.wait_ge(s["s0_free"], l + HEAD)
                sp.sem_inc(s["sp_passed"], 1)
                sp.dma_start(S0[:, B * H * P - 2 * T:], io["cos_sin"]).then_inc(s["cos_sin_landed"], 16)
                sp.dma_start(uext[:, :, PAD + NP:], io["pool_state"][l]).then_inc(s["ustate_landed"], 16)
                with sp.Fori(0, 6) as i:
                    for r in range(RING):
                        load(l, i * RING + (RING + r), r, l * UNITS + i * RING + (r + 1))
                sp.wait_ge(s["u_out"], (l + 1) * 16)
                sp.sem_inc(s["sp_passed"], 1)
                sp.wait_ge(s["qk_rope"], l + 1)
                sp.sem_inc(s["sp_passed"], 1)
                sp.wait_ge(s["pool_d"], (l + 1) * 8)
                sp.sem_inc(s["sp_passed"], 1)
                sp.wait_ge(s["pool_first"], (l + 1) * 2)
                sp.sem_inc(s["sp_passed"], 1)
                sp.dma_start(S0, io["s0"][l]).then_inc(s["s0_landed"], 16)
                with sp.Fori(0, 26) as i:
                    for r in range(RING):
                        load(l, i * RING + (28 + r), r, l * UNITS + i * RING + (25 + r))
                for u in (132, 133):
                    load(l, u, u % RING, l * UNITS + (u - RING + 1))
                for u in range(RING):
                    load(l + 1, u, u, l * UNITS + (UNITS - 1 if u == 0 else UNITS))
            pieces = ((0, 3), (3, 6), (6, KT - 1), (KT - 1, KT))
            for j0, j1 in pieces:
                sp.wait_ge(s["z_read_dve"], DEPTH * DVE_READS + HEAD - (KT - j1))
                sp.dma_start(io["y"][:, j0:j1], x[:, j0:j1]).then_inc(s["y_out"], 16)
            sp.wait_ge(s["y_out"], 16 * len(pieces))
            for r in range(RING):
                sp.wait_ge(ld[r], (DEPTH * PER_SLOT[r] + 1) * 16)

        @block.tensor
        def _(pe):
            def mm(out, a, b, start=True, stop=True, **kw):
                return nc.tensor.matmul(out, a, b, start=start, stop=stop, **kw)

            def product(outs, u, rhs_hi, rhs_lo, kk, have=None):
                for n, out in enumerate(outs):
                    for k in range(kk):
                        if have is not None and n == 0:
                            have(k)
                        hi = w_hi[:, u % RING].rearrange("p (k c) -> p k c", k=kk)[:, k, n * P:(n + 1) * P]
                        lo = w_lo[:, u % RING].rearrange("p (k c) -> p k c", k=kk)[:, k, n * P:(n + 1) * P]
                        mm(out, hi, rhs_hi(k), start=k == 0, stop=False)
                        mm(out, hi, rhs_lo(k), start=False, stop=False)
                        last = mm(out, lo, rhs_hi(k), start=False, stop=k == kk - 1)
                    if n < len(outs) - 1:
                        last.then_inc(s["half_done"], 1)
                last.then_inc(s["unit_done"], 1)

            def unit(l, u):
                pe.wait_ge(s["w_lo"], l * UNITS + (u + 1) + HEAD)
                if u < U_BR:
                    tiles = [u]
                elif u < U_O:
                    tiles = [T_BR + 2 * (u - U_BR), T_BR + 2 * (u - U_BR) + 1]
                else:
                    tiles = [T_O + u - U_O]
                for t4 in (t - 4 for t in tiles):
                    if t4 < 0:
                        pe.wait_ge(s["z_read_dve"], l * DVE_READS + HEAD)
                    elif U_GATE <= t4 < T_BR:
                        pe.wait_ge(s["z_read_act"], read_act(l, t4))
                    else:
                        pe.wait_ge(s["z_read_dve"], read_dve(l, t4))
                outs = [PZ[t % 4][:, 0:T] for t in tiles]
                if u < U_BR:
                    have = (lambda k: pe.wait_ge(s["a_lo"], l * 16 + (k + 1))) if u == 0 else None
                    product(outs, u, lambda k: a_hi[:, k], lambda k: a_lo[:, k], KT, have)
                elif u < U_O:
                    n, half = 2 - (u - U_BR) // 4, (u - U_BR) % 4
                    if half == 0:
                        if n == 2:
                            pe.wait_ge(s["oc_lo"], (l + 1) * G4)
                        elif n == 1:
                            pe.wait_ge(s["ob_lo"], (l + 1) * 4)
                        else:
                            pe.wait_ge(s["oa_lo"], l + 1 + HEAD)
                    hi, lo, o = ((a_hi, a_lo, 0), (h_hi, h_lo, 4), (h_hi, h_lo, 0))[n]
                    product(outs, u, lambda k: hi[:, o + k], lambda k: lo[:, o + k], 4)
                else:
                    have = (lambda k: pe.wait_ge(s["m_lo"], l * KT + (k + 1))) if u == U_O else None
                    product(outs, u, lambda k: h_hi[:, k], lambda k: h_lo[:, k], KT, have)

            def norm_sum(n):
                pe.wait_ge(s["consts_landed"], 16)
                pe.wait_ge(s["ssum"], n * KT + HEAD)
                mm(PM[3][:, 0:T], c("ones"), ssum).then_inc(s["nsum"], 1)

            def attention(l, u):
                kvr = [slice(0, HD), slice(HD, P)]
                qkv = qk.rearrange("p (j t) -> p j t", t=T)
                if u == 5:
                    pe.wait_ge(s["qk_sq"], l + 1)
                    for i in range(3):
                        last = mm(PM[i][:, 0:480], c("headones"), qk_rs[:, i * 480:(i + 1) * 480])
                    last.then_inc(s["qk_ss"], 1)
                if u == 6:
                    pe.wait_ge(s["z_read_dve"], read_dve(l, U_V))
                    pe.wait_ge(s["rstd"], 2 * l + 1)
                    for i, (o, n) in enumerate(((0, P), (P, P), (NP, NS))):
                        last = nc.tensor.transpose(PM[3][0:n, i * P:(i + 1) * P], vz[:, o:o + n], c("ident"))
                    last.then_inc(s["v_tr"], 1)
                if u == 9:
                    pe.wait_ge(s["qk_sin"], l + 1)
                    for i in range(3):
                        last = mm(PM[i][:, 0:480], c("perm"), sin_t[:, i * 480:(i + 1) * 480])
                    last.then_inc(s["qk_rot"], 1)
                if u == 11:
                    pe.wait_ge(s["qk_rope"], l + 1)
                    pe.wait_ge(s["v_tok"], 2 * l + 2)
                if u in (11, 13):
                    for g in ((0, 1, 2, 3) if u == 11 else (4, 5)):
                        if g >= 4:
                            pe.wait_ge(s["score_read"], l * 7 + (g - 3))
                        if g < 2:
                            for j in range(GRP):
                                last = mm(PM[g][:, j * P:(j + 1) * P], qkv[kvr[g], j, 0:P], qkv[kvr[g], 4, 0:P])
                        else:
                            kv, j0 = (g - 2) // 2, 2 * (g % 2)
                            for a in range(2):
                                last = mm(PM[g % 4][:, a * NP:(a + 1) * NP], qkv[kvr[kv], j0 + a, P:NP],
                                          qkv[kvr[kv], 4, 0:NP])
                        last.then_inc(s["score"], 1)
                if u == 14:
                    pe.wait_ge(s["score_read"], l * 7 + 3)
                    pe.wait_ge(s["q_samp"], 2 * l + 2)
                    pe.wait_ge(s["cache_landed"], 32 * (l + 1))
                    for g in range(2):
                        for b in range(4):
                            mm(PM[2][32 * b:32 * b + 32, g * SK:g * SK + P],
                               q_samp[:, (4 * g + b) * 32:(4 * g + b + 1) * 32], kcT[:, 4 * g + b])
                        last = mm(PM[2][:, g * SK + P:(g + 1) * SK], q_samp[:, g * P:(g + 1) * P],
                                  qkv[:, 4, NP:T])
                    last.then_inc(s["score"], 1)
                if u in (20, 21, 22):
                    for tg in {20: (0, 1), 21: (2, 3), 22: (4, 5)}[u]:
                        if tg < 4:
                            pe.wait_ge(s["oc_lo"], l * G4 + (tg + 1))
                        if tg < 2:
                            pe.wait_ge(s["prob_n"], l * 7 + (tg + 1))
                            src = [prob[:, tg, j * P:(j + 1) * P] for j in range(GRP)]
                        else:
                            kv, a = (tg - 2) // 2, tg % 2
                            pe.wait_ge(s["prob_n"], l * 7 + (4 + 2 * kv))
                            src = [prob[:, 2 + 2 * kv + j // 2, (j % 2) * NP + a * P:(j % 2) * NP + (a + 1) * P]
                                   for j in range(GRP)]
                        if tg >= 4:
                            pe.wait_ge(s["probT"], l * 8 + (tg - 3))
                        for j in range(GRP):
                            last = nc.tensor.transpose(PM[tg % 4][:, j * P:(j + 1) * P], src[j], c("ident"))
                        last.then_inc(s["prob_tr"], 1)
                if u == 22:
                    pe.wait_ge(s["prob_n"], l * 7 + 7)
                    pe.wait_ge(s["probT"], l * 8 + 3)
                    for g in range(2):
                        nc.tensor.transpose(PM[2][:, g * P:(g + 1) * P], p_samp[:, g, 0:P], c("ident"))
                        last = nc.tensor.transpose(PM[2][0:NS, (2 + g) * P:(3 + g) * P], p_samp[:, g, P:SK],
                                                   c("ident"))
                    last.then_inc(s["prob_tr"], 1)
                if u == 24:
                    pe.wait_ge(s["probT"], l * 8 + 8)
                    for kv in range(KV):
                        last = mm(PM[3][kvr[kv], :], v_tok[:, 0, kvr[kv]], probT[:, kv])
                    last.then_inc(s["pv"], 1)
                    for kv in range(KV):
                        mm(PM[0][kvr[kv], :], v_tok[:, 0, kvr[kv]], probT[:, 2 + 2 * kv], stop=False)
                        last = mm(PM[0][kvr[kv], :], v_tok[:, 1, kvr[kv]], probT[:, 3 + 2 * kv], start=False)
                    last.then_inc(s["pv"], 1)
                    mm(PM[1][:, 0:2 * P], v_tok[0:NS, 2], pnT[0:NS], skip_group_check=True)
                    for b in range(B):
                        last = mm(PM[1][:, b * 32:(b + 1) * 32], vc[:, b],
                                  psT[:, b // 4, (b % 4) * 32:(b % 4 + 1) * 32], start=False,
                                  skip_group_check=True)
                    last.then_inc(s["pv"], 1)

            def pooling(l, u):
                if u == 18:
                    pe.wait_ge(s["pool_d"], (l + 1) * 8)
                    pe.wait_ge(s["pool_first"], (l + 1) * 2)
                    pe.wait_ge(s["poolw_landed"], (l + 1) * 16)
                    pe.wait_ge(s["score_read"], (l + 1) * 7)
                    for g in range(G4):
                        last = mm(PM[g][:, 0:T], poolw[:, g], pool_d[:, g])
                    last.then_inc(s["pool_y"], 1)

            def diag_sample(xk, xq, bank):
                for h in range(H):
                    last = mm(bank[0:NS, h * NS:(h + 1) * NS], hv(xk)[:, h, NP:T], hv(xq)[:, h, NP:T])
                return last

            def hgrn(l, u):
                if u == 28:
                    pe.wait_ge(s["ob_lo"], (l + 1) * 4)
                    pe.wait_ge(s["z_read_dve"], read_dve(l, U_HI + 3))
                    for h in range(H):
                        for n in range(3):
                            w = P if n < 2 else NS
                            last = nc.tensor.transpose(PM[n][0:w, h * P:(h + 1) * P],
                                                       hv(ZI)[:, h, n * P:n * P + w], c("ident"))
                    last.then_inc(s["i_tr"], 1)
                if u == 30:
                    pe.wait_ge(s["KE"], l + 1)
                    pe.wait_ge(s["QE"], l + 1)
                    pe.wait_ge(s["itok"], 2 * l + 2)
                    for h in range(H):
                        for n in range(3):
                            w = P if n < 2 else NS
                            last = nc.tensor.transpose(PM[n][0:w, h * P:(h + 1) * P],
                                                       hv(X1)[:, h, n * P:n * P + w], c("ident"))
                    last.then_inc(s["k_tr"], 1)
                    for h in range(H):
                        last = mm(PM[3][:, h * P:(h + 1) * P], hv(X1)[:, h, 0:P], hv(ZF)[:, h, P:NP])
                    last.then_inc(s["cross"], 1)
                if u == 32:
                    pe.wait_ge(s["ktok"], 2 * l + 2)
                    for n in range(NB):
                        for h in range(H):
                            last = mm(PM[n][:, h * P:(h + 1) * P], ktok4[:, n, h], itok[:, n, h])
                    last.then_inc(s["sfin"], 1)
                    pe.wait_ge(s["AC"], l + 1)
                    for n in range(NB):
                        for h in range(H):
                            last = mm(PM[2 + n][:, h * P:(h + 1) * P], hv(KK)[:, h, n * P:(n + 1) * P],
                                      hv(ZQ)[:, h, n * P:(n + 1) * P])
                    last.then_inc(s["level_mm"], 1)
                if u == 34:
                    pe.wait_ge(s["level_read"], 11 * l + 1)
                    diag_sample(KK, ZQ, PM[2]).then_inc(s["level_mm"], 1)
                if 34 <= u <= 46 and u % 2 == 0:
                    i = (u - 34) // 2
                    X = (X0, X1)[i % 2]
                    m = LEVELS[i]
                    pe.wait_ge(s["level_x"], 14 * l + 2 * (i + 1))
                    if i == 0:
                        pe.wait_ge(s["sfin_read"], l + 1)
                    if i >= 2:
                        pe.wait_ge(s["level_read"], 11 * l + (i + 1))
                    for n in range(NB):
                        for h in range(H):
                            xs = hv(X)[:, h, n * P:(n + 1) * P]
                            late = xs.rearrange("p (a e s) -> p a e s", e=2, s=m)[:, :, 1, :]
                            o = (n * H + h) * (P // 2)
                            last = mm(PM[i % 2][:, o:o + P // 2].rearrange("p (a s) -> p a s", s=m), xs, late)
                    last.then_inc(s["level_mm"], 1)
                    if i >= 5:
                        pe.wait_ge(s["level_read"], 11 * l + (2 if i == 5 else 9))
                        diag_sample(X, X, PM[2]).then_inc(s["level_mm"], 1)
                if u in (35, 37, 39, 41):
                    if u == 35:
                        pe.wait_ge(s["s0_landed"], 16 * (l + 1))
                        pe.wait_ge(s["level_read"], 11 * l + 1)
                    h = (u - 35) // 2
                    for b in range(B):
                        o = h * NS + b * TS
                        last = mm(PM[3][:, o:o + TS], S0v[:, b, h], hv(ZF)[:, h, NP + b * TS:NP + (b + 1) * TS],
                                  start=h == 0 and b == 0, skip_group_check=True)
                    last.then_inc(s["s0_q"], 1)
                if u == 48:
                    pe.wait_ge(s["level_read"], 11 * l + 11)
                    for h in range(H):
                        last = mm(PM[0][:, h * P:(h + 1) * P], itok[:, 0, h], AT[:, 0, h])
                    last.then_inc(s["o_ps"], 1)
                    for h in range(H):
                        mm(PM[1][:, h * P:(h + 1) * P], itok[:, 0, h], ACv[:, h], stop=False)
                        last = mm(PM[1][:, h * P:(h + 1) * P], itok[:, 1, h], AT[:, 1, h], start=False)
                    last.then_inc(s["o_ps"], 1)
                    for h in range(H):
                        last = mm(PM[3][:, h * NS:(h + 1) * NS], itok[0:NS, 2, h], ATsv[0:NS, h],
                                  start=False, skip_group_check=True)
                    last.then_inc(s["o_ps"], 1)
                if u == 50:
                    pe.wait_ge(s["o_sq"], l + 1)
                    for i in range(3):
                        last = mm(PM[i][:, 0:384], c("ones"), D0[:, i * 384:(i + 1) * 384])
                    last.then_inc(s["o_ss"], 1)
                if 53 <= u <= 56:
                    h = u - 53
                    if h < 2:
                        pe.wait_ge(s["o_rstd"], l + 1)
                    else:
                        pe.wait_ge(s["snew_read"], 4 * l + (h - 1) + HEAD)
                    pe.wait_ge(s["imask"], 4 * l + (h + 1))
                    im = (KK, D1, X1, ZF)[h]
                    for half in range(2):
                        last = mm(PM[2 * (h % 2) + half], ktok_s[0:NS, h], im[0:NS, half * 512:(half + 1) * 512])
                    last.then_inc(s["snew"], 1)

            def ffn_turn(l, i, first=False):
                for j in range(16):
                    u = U_FFN + j
                    pe.wait_ge(s["w_lo"], l * UNITS + i * 16 + (u + 1) + HEAD)
                    pe.wait_ge(s["z_read_dve"], i * 16 + read_dve(l, T_FFN + j - 4))
                    out = [PZ[(T_FFN + j) % 4][:, 0:T]]
                    if j < 8:
                        have = (lambda k: pe.wait_ge(s["a_lo"], l * 16 + (9 + k))) if first and j == 0 else None
                        product(out, u, lambda k: a_hi[:, k], lambda k: a_lo[:, k], KT, have)
                    else:
                        have = (lambda k: pe.wait_ge(s["f_lo"], l * 8 * FI + i * 8 + (k + 1) + HEAD)) if j == 8 else None
                        product(out, u, lambda k: h_hi[:, k], lambda k: h_lo[:, k], KT, have)
                    if first and j == 0:
                        pe.wait_ge(s["snew_read"], 4 * l + 4 + HEAD)
                        norm_sum(2 * l + 2)

            for name in ("unit_done", "nsum", "pool_y"):
                pe.sem_inc(s[name], HEAD)
            with pe.Fori(0, DEPTH) as l:
                for u in range(U_FFN):
                    unit(l, u)
                    if u == 0:
                        norm_sum(2 * l + 1)
                    attention(l, u)
                    pooling(l, u)
                    hgrn(l, u)
                ffn_turn(l, 0, first=True)
                with pe.Fori(0, FI - 1) as i:
                    ffn_turn(l, i + 1)

        @block.scalar
        def _(act):
            chain = Chain(act, "act_chain", 6)
            act_fn = nc.scalar.activation
            one, eps = c("one"), c("eps")

            def load_ln_exp():
                nc.scalar.preload_act_table_set("natural_log_exp_and_others")

            def split(l, u, i=0, slot_is_new=False):
                r = u % RING
                act.wait_ge(ld[r], slot_landed(u, l, i))
                if not slot_is_new:
                    before = -1 if u == 0 else 0 if u < RING else u - RING + 1
                    act.wait_ge(s["unit_done"], l * UNITS + i * 16 + before + HEAD)
                act_fn(w_hi[:, r], raw[:, r], ACT.Copy).then_inc(s["w_hi"], 1)

            def next_input(n, j, ready, weight):
                act.wait_ge(s["z_read_dve"], ready)
                input_hi(j, weight)
                square(n, j)

            def input_hi(j, weight):
                act_fn(a_hi[:, j], x[:, j], ACT.Copy, scale=weight(j)).then_inc(s["a_hi"], 1)

            def square(n, j):
                act.wait_ge(s["ssum"], (n - 1) * KT + max(j - 1, 0) + HEAD)
                act_fn(sq[:, j % 2], x[:, j], ACT.Square).then_inc(s["x_sq"], 1)

            def norm(n):
                act.wait_ge(s["nsum"], n + HEAD)
                chain(act_fn(rstd[:], PM[3][:, 0:T], ACT.Ln, bias=eps, scale=1.0 / D_MODEL))
                act_fn(rstd[:], rstd[:], ACT.Exp, scale=-0.5).then_inc(s["rstd"], 1)

            def read_gate(l, t):
                act.wait_ge(s["unit_done"], l * UNITS + (t + 1) + HEAD)
                act_fn(gate_tile(t), PZ[t % 4][:, 0:T], ACT.Copy).then_inc(s["z_read_act"], 1)

            def attention(l, u):
                if u == 4:
                    act.wait_ge(s["z_read_dve"], read_dve(l, U_K))
                    act_fn(qk_rs, qk, ACT.Square).then_inc(s["qk_sq"], 1)
                if u == 6:
                    act.wait_ge(s["qk_ss"], l + 1)
                    r3 = qk_rs.rearrange("p (b n) -> p b n", b=3)
                    chain(act_fn(r3, pm[:, 0:3, 0:480], ACT.Ln, bias=eps, scale=1.0 / HD))
                    act_fn(qk_rs, qk_rs, ACT.Exp, scale=-0.5).then_inc(s["qk_rstd"], 1)
                if u == 7:
                    act.wait_ge(s["v_tr"], l + 1)
                    act_fn(v_tok[:, 0:2], PM[3][:, 0:256].rearrange("p (b n) -> p b n", b=2),
                           ACT.Copy).then_inc(s["v_tok"], 1)
                    act_fn(v_tok[0:NS, 2], PM[3][0:NS, 256:384], ACT.Copy).then_inc(s["v_tok"], 1)
                if u == 16:
                    act.wait_ge(s["negm"], l + 1)
                    act_fn(es_, se, ACT.Exp).then_inc(s["sink_e"], 1)
                for g in {16: (0, 1), 17: (2, 3, 4, 5, 6)}.get(u, ()):
                    heads = GRP if g < 2 else 2
                    for a in range(heads):
                        col = g * 4 + a if g < 2 else 8 + 2 * (g - 2) + a
                        if g < 6:
                            w = 512 // heads
                            pg = prob[:, g, a * w:(a + 1) * w]
                        else:
                            pg = p_samp[:, a]
                        last = act_fn(pg, pg, ACT.Exp, bias=negm[:, col:col + 1], accum_out=sm[:, col:col + 1])
                        last.then_inc(s["prob_e"], 1)
                for tg in {21: (0, 1), 22: (2, 3), 23: (4, 5)}.get(u, ()):
                    act.wait_ge(s["prob_tr"], 7 * l + (tg + 1))
                    act_fn(probT[:, tg], PM[tg % 4], ACT.Copy).then_inc(s["probT"], 1)
                if u == 23:
                    act.wait_ge(s["prob_tr"], 7 * l + 7)
                    act_fn(psT, PM[2][:, 0:256].rearrange("p (g n) -> p g n", g=2), ACT.Copy).then_inc(s["probT"], 1)
                    act_fn(pnT[0:NS], PM[2][0:NS, 256:512].rearrange("p (g n) -> p g n", g=2),
                           ACT.Copy).then_inc(s["probT"], 1)
                if u == 25:
                    for n in range(2):
                        act.wait_ge(s["pv"], 3 * l + (n + 1))
                        act_fn(h_hi[:, 4:8, n * P:(n + 1) * P], PM[3 - 3 * n].rearrange("p (j t) -> p j t", j=4),
                               ACT.Copy).then_inc(s["ob_hi"], 1)
                    act.wait_ge(s["pv"], 3 * l + 3)
                    for kv in range(KV):
                        o, z = samp_out(h_hi, kv)
                        act_fn(o, z, ACT.Copy).then_inc(s["ob_hi"], 1)

            def pooling(l, u):
                if u == 19:
                    act.wait_ge(s["pool_y"], l + 1 + HEAD)
                    for g in range(G4):
                        act_fn(h_hi[:, g], PM[g][:, 0:T], ACT.Copy, scale=pr("pscale", g)).then_inc(s["oc_hi"], 1)

            def hgrn(l, u):
                if u == 20:
                    act.wait_ge(s["hz_abs"], l + 1)
                    chain(act_fn(GG, GG, ACT.Exp, scale=-1.0))
                    act_fn(GG, GG, ACT.Ln, bias=one).then_inc(s["hz_ln1"], 1)
                if u == 23:
                    act.wait_ge(s["hz_dif"], l + 1)
                    chain(act_fn(GG, GG, ACT.Exp))
                    act_fn(GG, GG, ACT.Ln, bias=one).then_inc(s["hz_ln2"], 1)
                if u == 26:
                    act.wait_ge(s["kv_out"], 32 * (l + 1))
                    act.wait_ge(s["end_g"], 2 * l + 2)
                    act_fn(X0, GG, ACT.Exp).then_inc(s["E0"], 1)
                    act_fn(X1, X1, ACT.Exp).then_inc(s["E1"], 1)
                    nc.scalar.preload_act_table(ACT.Sigmoid)
                    act.wait_ge(s["z_read_dve"], read_dve(l, U_HG + 3))
                    act_fn(D0, ZQ, ACT.Sigmoid).then_inc(s["sig"], 1)
                if u == 27:
                    act_fn(KK, ZF, ACT.Sigmoid, scale=-1.0).then_inc(s["sig"], 1)
                if u == 28:
                    act.wait_ge(s["i_tr"], l + 1)
                    act_fn(itok[:, 0:2], pm[:, 0:2].rearrange("p b (h n) -> p b h n", h=H),
                           ACT.Copy).then_inc(s["itok"], 1)
                    act_fn(itok[0:NS, 2], PM[2][0:NS].rearrange("p (h n) -> p h n", h=H),
                           ACT.Copy).then_inc(s["itok"], 1)
                if u == 29:
                    act_fn(D1, ZG, ACT.Sigmoid).then_inc(s["sig"], 1)
                    load_ln_exp()
                if u == 31:
                    act.wait_ge(s["k_tr"], l + 1)
                    act_fn(ktok4, pm[:, 0:2].rearrange("p b (h n) -> p b h n", h=H), ACT.Copy).then_inc(s["ktok"], 1)
                    act_fn(ktok_s[0:NS], PM[2][0:NS].rearrange("p (h n) -> p h n", h=H),
                           ACT.Copy).then_inc(s["ktok"], 1)
                    act.wait_ge(s["cross"], l + 1)
                    act_fn(AC, PM[3], ACT.Copy).then_inc(s["AC"], 1)
                if 32 <= u <= 44 and u % 2 == 0:
                    i = (u - 32) // 2
                    D = hv((D0, D1)[i % 2])
                    w = T if LEVELS[i] <= 2 else NP
                    act.wait_ge(s["level_d"], 14 * l + 2 * (i + 1))
                    act_fn(D[:, :, 0:w], D[:, :, 0:w], ACT.Exp).then_inc(s["level_e"], 1)
                if u == 49:
                    act.wait_ge(s["sp_out"], 16 * (l + 1))
                    for n in range(2):
                        act.wait_ge(s["o_ps"], 3 * l + (n + 1))
                        act_fn(hv(ZI)[:, :, n * P:(n + 1) * P], PM[n].rearrange("p (h t) -> p h t", h=H),
                               ACT.Copy).then_inc(s["o_sb"], 1)
                    act.wait_ge(s["o_ps"], 3 * l + 3)
                    act_fn(hv(ZI)[:, :, NP:T], PM[3][:, 0:H * NS].rearrange("p (h t) -> p h t", h=H),
                           ACT.Copy).then_inc(s["o_sb"], 1)
                    act.wait_ge(s["o_sb"], 3 * l + 3)
                    act_fn(D0, ZI, ACT.Square).then_inc(s["o_sq"], 1)
                if u in (46, 47, 50):
                    if u == 46:
                        nc.scalar.preload_act_table(ACT.Sigmoid)
                    n = {46: 2, 47: 1, 50: 0}[u]
                    act.wait_ge(s["gate_z"], 3 * l + (3 - n))
                    act_fn(gates[:, n], gates[:, n], ACT.Sigmoid).then_inc(s["gate"], 1)
                    if u == 50:
                        load_ln_exp()
                if u == 51:
                    act.wait_ge(s["o_ss"], l + 1)
                    chain(act_fn(GG.rearrange("p (b n) -> p b n", b=3), pm[:, 0:3, 0:384], ACT.Ln, bias=eps,
                                 scale=1.0 / P))
                    act_fn(GG, GG, ACT.Exp, scale=-0.5).then_inc(s["o_rstd"], 1)
                if u == 53:
                    act.wait_ge(s["oa"], l + 1)
                    act_fn(a_hi[:, 0:4], hv(X0), ACT.Copy).then_inc(s["oa_hi"], 1)

            def mlp(l, i, last):
                for j in range(16):
                    if j + LEAD < 16 or not last:
                        split(l, U_FFN + j + LEAD, i)
                    if j < 8:
                        act.wait_ge(s["z_read_dve"], i * 16 + read_dve(l, T_FFN + j))
                        act.wait_ge(s["f_lo"], l * 8 * FI + i * 8 + max(j - 1, 0) + HEAD)
                        act_fn(hsq[:, j % 2], relu[:, j % 2], ACT.Square).then_inc(s["hsq"], 1)
                        act.wait_ge(s["hsq"], l * 8 * FI + i * 8 + (j + 1) + HEAD)
                        act_fn(h_hi[:, j], hsq[:, j % 2], ACT.Copy).then_inc(s["f_hi"], 1)
                    if last and j == 15:
                        split(l + 1, 0)
                    if last and j >= 8:
                        next_input(2 * l + 3, j - 8, i * 16 + read_dve(l, T_FFN + j), lambda k: pr("norm_next", k))
                if last:
                    for u in range(1, LEAD):
                        split(l + 1, u)

            load_ln_exp()
            act.wait_ge(s["prep_v"], 1)
            act_fn(small[:, 0:2 * H], small[:, 0:2 * H], ACT.Exp).then_inc(s["prep_a"], 1)
            act.wait_ge(s["prep_v"], 2)
            act_fn(small[:, 32:56], small[:, 32:56], ACT.Ln).then_inc(s["prep_a"], 1)
            for j in range(KT):
                if j % 4 == 0:
                    act.wait_ge(s[f"x_landed{j}"], 16)
                input_hi(j, first_norm)
                if j == 3:
                    split(0, 0, slot_is_new=True)
            split(0, 1, slot_is_new=True)
            for j in range(KT):
                square(1, j)
            split(0, 2, slot_is_new=True)
            act.wait_ge(s["consts_landed"], 16)
            with act.Fori(0, DEPTH) as l:
                chain.layer(l * chain.per_layer)
                for u in range(U_FFN):
                    split(l, u + LEAD)
                    if u == 0:
                        norm(2 * l + 1)
                    if U_GATE <= u < U_BR:
                        read_gate(l, u)
                    if u >= U_O:
                        next_input(2 * l + 2, u - U_O, read_dve(l, T_O + u - U_O), lambda k: pr("norm_ffn", k))
                    if U_BR + 8 <= u < U_O:
                        for d in (2 * (u - U_BR - 8), 2 * (u - U_BR - 8) + 1):
                            if d < KT - 2:
                                act.wait_ge(s["merged"], l * (KT - 2) + (d + 1))
                            else:
                                act.wait_ge(s["merged_late"], l * 2 + (d - KT + 3))
                            act_fn(h_hi[:, d], gates[:, 2, d], ACT.Copy).then_inc(s["m_hi"], 1)
                    attention(l, u)
                    pooling(l, u)
                    hgrn(l, u)
                norm(2 * l + 2)
                with act.Fori(0, FI - 1) as i:
                    mlp(l, i, False)
                mlp(l, FI - 1, True)
                chain.close()

        @block.vector
        def _(dve):
            chain = Chain(dve, "dve_chain", 0)
            tt, ts_, stt = nc.vector.tensor_tensor, nc.vector.tensor_scalar, nc.vector.scalar_tensor_tensor
            f = lambda a: a.bitcast(F32)

            def split(l, u, i=0):
                dve.wait_ge(s["w_hi"], l * UNITS + i * 16 + (u + 1))
                r = u % RING
                tt(w_lo[:, r], raw[:, r], f(w_hi[:, r]), ALU.subtract).then_inc(s["w_lo"], 1)

            def add_square(n, j):
                dve.wait_ge(s["x_sq"], (n - 1) * KT + (j + 1))
                if j == 0:
                    dve.wait_ge(s["nsum"], n - 1 + HEAD)
                    nc.vector.tensor_copy(ssum, sq[:, 0]).then_inc(s["ssum"], 1)
                else:
                    dve.wait_ge(s["ssum"], (n - 1) * KT + j + HEAD)
                    tt(ssum, ssum, sq[:, j % 2], ALU.add).then_inc(s["ssum"], 1)

            def input_lo(n, j, weight):
                dve.wait_ge(s["a_hi"], (n - 1) * KT + (j + 1))
                stt(a_lo[:, j], x[:, j], weight(j), f(a_hi[:, j]), ALU.mult, ALU.subtract).then_inc(s["a_lo"], 1)

            def read_tile(l, t):
                dve.wait_ge(s["unit_done"], l * UNITS + (t + 1) + HEAD)
                if t == 0:
                    dve.wait_ge(s["rstd"], 2 * l + 1)
                z = PZ[t % 4][:, 0:T]
                if U_U <= t < U_HF:
                    g = t - U_U
                    if g == 0:
                        dve.wait_ge(s["s0_free"], l + HEAD)
                    tt(uext[:, g, PAD:PAD + NP], z[:, 0:NP], rstd[:, 0:NP], ALU.mult)
                    out = uext[:, g, PAD + NP:].rearrange("p (b n) -> p b n", n=SEG)[:, :, PAD:]
                    if g == 0:
                        dve.wait_ge(s["ustate_landed"], 16 * (l + 1))
                    tt(out, samp(z[:, NP:T]), samp(rstd[:, NP:T]), ALU.mult).then_inc(s["z_read_dve"], 1)
                    return
                if t <= U_K:
                    out = qk[:, t * T:(t + 1) * T]
                elif t == U_V:
                    out = vz
                else:
                    base, first_u = ((ZF, U_HF), (ZQ, U_HQ), (ZI, U_HI), (ZG, U_HG))[(t - U_HF) // 4]
                    out = hv(base)[:, t - first_u]
                tt(out, z, rstd[:], ALU.mult).then_inc(s["z_read_dve"], 1)

            def add_to_x(l, j, z, unit_done):
                dve.wait_ge(s["unit_done"], unit_done + HEAD)
                tt(x[:, j], x[:, j], z[:, 0:T], ALU.add).then_inc(s["z_read_dve"], 1)

            def attention(l, u):
                if u == 7:
                    dve.wait_ge(s["qk_rstd"], l + 1)
                    stt(qk[:, 0:4 * T], qk[:, 0:4 * T], pr("qw"), qk_rs[:, 0:4 * T], ALU.mult,
                        ALU.mult).then_inc(s["qk_norm"], 1)
                    stt(qk[:, 4 * T:], qk[:, 4 * T:], pr("kw"), qk_rs[:, 4 * T:], ALU.mult,
                        ALU.mult).then_inc(s["qk_norm"], 1)
                    dve.wait_ge(s["qk_norm"], 2 * l + 2)
                    dve.wait_ge(s["cos_sin_landed"], 16 * (l + 1))
                    tt(sin_t.rearrange("p (j t) -> p j t", j=5), qk.rearrange("p (j t) -> p j t", j=5), bc(sin, 5),
                       ALU.mult).then_inc(s["qk_sin"], 1)
                if u == 10:
                    dve.wait_ge(s["qk_rot"], l + 1)
                    dve.wait_ge(s["qk_cos"], l + 1)
                    b3 = lambda a: a.rearrange("p (b n) -> p b n", b=3)
                    tt(b3(qk), b3(qk_rs), pm[:, 0:3, 0:480], ALU.add).then_inc(s["qk_rope"], 1)
                for g in {12: (0, 1), 13: (2, 3), 14: (4, 5)}.get(u, ()):
                    dve.wait_ge(s["score"], 7 * l + (g + 1))
                    hs = GRP if g < 2 else 2
                    mask = bc(c("mask_prev")[:, P:] if g < 2 else c("mask_prev"), hs)
                    pv = prob[:, g].rearrange("p (a n) -> p a n", a=hs)
                    stt(pv, PM[g % 4].rearrange("p (a n) -> p a n", a=hs), HD ** -0.5, mask, ALU.mult,
                        ALU.add).then_inc(s["score_read"], 1)
                    dve.wait_ge(s["score_read"], 7 * l + (g + 1))
                    o = g * 4 if g < 2 else 8 + 2 * (g - 2)
                    last = nc.vector.reduce_max(mx[:, o:o + hs], pv, AX_X)
                    last.then_inc(s["score_max"], 1)
                if u == 15:
                    dve.wait_ge(s["score"], 7 * l + 7)
                    stt(p_samp, PM[2][:, 0:2 * SK].rearrange("p (g n) -> p g n", g=2), HD ** -0.5,
                        c("mask_samp").rearrange("p (g n) -> p g n", g=2), ALU.mult,
                        ALU.add).then_inc(s["score_read"], 1)
                    dve.wait_ge(s["score_read"], 7 * l + 7)
                    nc.vector.reduce_max(mx[:, 16:18], p_samp, AX_X).then_inc(s["score_max"], 1)
                    dve.wait_ge(s["score_max"], 7 * l + 7)
                    sink2 = bc(pr("sink", 0, 8), 2)
                    v16 = lambda a: a[:, 0:16].rearrange("p (n h) -> p n h", n=2)
                    chain(tt(v16(mx), v16(mx), sink2, ALU.max))
                    chain(ts_(mx[:, 16:18], mx[:, 16:18], pr("sink_s"), None, ALU.max))
                    chain(ts_(negm, mx, -1.0, None, ALU.mult))
                    chain(tt(v16(se), v16(negm), sink2, ALU.add))
                    ts_(se[:, 16:18], negm[:, 16:18], pr("sink_s"), None, ALU.add).then_inc(s["negm"], 1)
                if u == 18:
                    dve.wait_ge(s["prob_e"], 18 * (l + 1))
                    dve.wait_ge(s["sink_e"], l + 1)
                    chain(tt(den, sm, es_, ALU.add))
                    nc.vector.reciprocal(rec, den).then_inc(s["rec"], 1)
                if u == 25:
                    for n in range(2):
                        dve.wait_ge(s["ob_hi"], 4 * l + (n + 1))
                        tt(h_lo[:, 4:8, n * P:(n + 1) * P], PM[3 - 3 * n].rearrange("p (j t) -> p j t", j=4),
                           f(h_hi[:, 4:8, n * P:(n + 1) * P]), ALU.subtract).then_inc(s["ob_lo"], 1)
                    for kv in range(KV):
                        dve.wait_ge(s["ob_hi"], 4 * l + (kv + 3))
                        o, z = samp_out(h_lo, kv)
                        tt(o, z, f(samp_out(h_hi, kv)[0]), ALU.subtract).then_inc(s["ob_lo"], 1)

            def pooling(l, u):
                if u == 16:
                    dve.wait_ge(s["wsum"], l + 1)
                    for g, w in enumerate(WINDOWS):
                        stt(pool_d[:, g, PAD:NP], wsum[g][:, 2 * PAD:PAD + NP], 1.0 / w, uext[:, g, 2 * PAD:PAD + NP],
                            ALU.mult, ALU.subtract).then_inc(s["pool_d"], 1)
                        v = lambda a: a[:, PAD + NP:].rearrange("p (b n) -> p b n", n=SEG)[:, :, PAD:]
                        stt(samp(pool_d[:, g, NP:T]), v(wsum[g]), 1.0 / w, v(uext[:, g]), ALU.mult,
                            ALU.subtract).then_inc(s["pool_d"], 1)
                if u == 19:
                    for g in range(G4):
                        dve.wait_ge(s["oc_hi"], G4 * l + (g + 1))
                        stt(h_lo[:, g], PM[g][:, 0:T], pr("pscale", g), f(h_hi[:, g]), ALU.mult,
                            ALU.subtract).then_inc(s["oc_lo"], 1)

            def hgrn(l, u):
                if u == 19:
                    dve.wait_ge(s["pool_y"], l + 1 + HEAD)
                    dve.wait_ge(s["z_read_dve"], read_dve(l, U_HF + 3))
                    stt(GG, ZF, -1.0, ZF, ALU.mult, ALU.max).then_inc(s["hz_abs"], 1)
                if u == 21:
                    dve.wait_ge(s["hz_ln1"], l + 1)
                    chain(stt(GG, ZF, 0.0, GG, ALU.min, ALU.subtract))
                    for h in range(H):
                        last = ts_(hv(LF)[:, h], hv(GG)[:, h], pr("log_om", h), pr("log_lb", h), ALU.add, ALU.max)
                    chain(last)
                if u == 22:
                    for h in range(H):
                        last = ts_(hv(GG)[:, h], hv(GG)[:, h], pr("log_om", h), pr("log_lb", h), ALU.add, ALU.min)
                    chain(last)
                    tt(GG, GG, LF, ALU.subtract).then_inc(s["hz_dif"], 1)
                if u == 24:
                    dve.wait_ge(s["hz_ln2"], l + 1)
                    chain(tt(LF, LF, GG, ALU.add))
                    for h in range(H):
                        last = nc.vector.tensor_tensor_scan(hv(GG)[:, h], c("seg"), hv(LF)[:, h], 0.0, ALU.mult,
                                                            ALU.add)
                    chain(last)
                if u == 25:
                    dve.wait_ge(s["kv_out"], 32 * (l + 1))
                    dve.wait_ge(s["ob_hi"], 4 * (l + 1))
                    x1 = hv(X1)
                    g2 = hv(GG)[:, :, 0:NP].rearrange("p h (n t) -> p h n t", n=NB)
                    d2 = x1[:, :, 0:NP].rearrange("p h (n t) -> p h n t", n=NB)
                    tt(d2, g2[:, :, :, P - 1:P].to_broadcast([P, H, NB, P]), g2,
                       ALU.subtract).then_inc(s["end_g"], 1)
                    g3 = hv(GG)[:, :, NP:T].rearrange("p h (b t) -> p h b t", t=TS)
                    d3 = x1[:, :, NP:T].rearrange("p h (b t) -> p h b t", t=TS)
                    tt(d3, g3[:, :, :, TS - 1:TS].to_broadcast([P, H, B, TS]), g3,
                       ALU.subtract).then_inc(s["end_g"], 1)
                if u == 27:
                    dve.wait_ge(s["sig"], 3 * l + 2)
                    for h in range(H):
                        last = ts_(hv(KK)[:, h], hv(KK)[:, h], pr("om", h), None, ALU.mult)
                    last.then_inc(s["hz_k"], 1)
                    dve.wait_ge(s["E1"], l + 1)
                    dve.wait_ge(s["hz_k"], l + 1)
                    tt(X1, KK, X1, ALU.mult).then_inc(s["KE"], 1)
                if u == 28:
                    dve.wait_ge(s["hz_q"], l + 1)
                    tt(ZF, ZQ, X0, ALU.mult).then_inc(s["QE"], 1)
                    nc.vector.tensor_copy(ep, hv(X0)[:, :, NP - 1:NP].rearrange("p h o -> p (h o)"))
                    nc.vector.tensor_copy(es.rearrange("p (b h) -> p h b", b=B),
                                          hv(X0)[:, :, NP + TS - 1:T:TS]).then_inc(s["ends"], 1)
                if u == 33:
                    dve.wait_ge(s["sfin"], l + 1)
                    dve.wait_ge(s["ends"], l + 1)
                    dve.wait_ge(s["i_tr"], l + 1)
                    for h in range(H):
                        last = ts_(ZI[:, h * P:(h + 1) * P], PM[0][:, h * P:(h + 1) * P], ep[:, h:h + 1], None,
                                   ALU.mult)
                    chain(last)
                    tt(ZI[:, 0:512], ZI[:, 0:512], PM[1], ALU.add).then_inc(s["sfin_read"], 1)
                    dve.wait_ge(s["at_zero"], 2 * l + 2)
                    keep_diagonal(l)
                if 32 <= u <= 44 and u % 2 == 0:
                    i = (u - 32) // 2
                    m = LEVELS[i]
                    D = (D0, D1)[i % 2]
                    if i == 1:
                        dve.wait_ge(s["silu_g"], l + 1)
                    if i >= 2:
                        dve.wait_ge(s["level_x"], 14 * l + 2 * (i - 1))
                    g0, g1 = level_views(GG, m)
                    d0, d1 = level_views(D, m)
                    ref = g0[:, :, :, m - 1:m].to_broadcast(list(g0.shape))
                    tt(d0, ref, g0, ALU.subtract).then_inc(s["level_d"], 1)
                    tt(d1, g1, ref, ALU.subtract).then_inc(s["level_d"], 1)
                if 33 <= u <= 45 and u % 2:
                    i = (u - 33) // 2
                    m = LEVELS[i]
                    D = (D0, D1)[i % 2]
                    X = (X0, X1)[i % 2]
                    dve.wait_ge(s["level_e"], 7 * l + (i + 1))
                    if i == 0:
                        dve.wait_ge(s["ends"], l + 1)
                    if i == 1:
                        dve.wait_ge(s["cross"], l + 1)
                    if i >= 2:
                        dve.wait_ge(s["level_mm"], 11 * l + (i + 1))
                    d0, d1 = level_views(D, m)
                    x0, x1 = level_views(X, m)
                    tt(x0, level_views(KK, m)[0], d0, ALU.mult).then_inc(s["level_x"], 1)
                    tt(x1, level_views(ZQ, m)[1], d1, ALU.mult).then_inc(s["level_x"], 1)
                if u == 35:
                    keep_sample(l, 2, len(LEVELS), 2)
                if 35 <= u <= 47 and u % 2:
                    i = (u - 35) // 2
                    keep(l, (3 + i) if i < 6 else 10, i, i % 2)
                    if i == 5:
                        keep_sample(l, 9, 5, 2)
                    if i == 6:
                        keep_sample(l, 11, 6, 2)
                if u == 52:
                    dve.wait_ge(s["o_rstd"], l + 1)
                    dve.wait_ge(s["o_sb"], 3 * l + 3)
                    chain(stt(X0, ZI, pr("onorm"), GG, ALU.mult, ALU.mult))
                    tt(X0, X0, ZG, ALU.mult).then_inc(s["oa"], 1)
                if u == 53:
                    dve.wait_ge(s["oa_hi"], l + 1)
                    tt(a_lo[:, 0:4], hv(X0), f(a_hi[:, 0:4]), ALU.subtract).then_inc(s["oa_lo"], 1)
                if 54 <= u <= 57:
                    h = u - 54
                    dve.wait_ge(s["snew"], 4 * l + (h + 1))
                    dve.wait_ge(s["s0_decay"], l + 1)
                    b0 = 2 * (h % 2)
                    tt(S0v[:, :, h], S0v[:, :, h],
                       pm[:, b0:b0 + 2].rearrange("p c (b n) -> p (c b) n", n=P), ALU.add).then_inc(s["snew_read"], 1)

            def keep_diagonal(l):
                dve.wait_ge(s["level_mm"], 11 * l + 1)
                dve.sem_inc(s["dve_passed"], 1)
                dve.wait_ge(s["lmask_ready"], 1)
                for n in range(NB):
                    last = nc.vector.copy_predicated(AT[:, n], bc(lmask[:, len(LEVELS)], H),
                                                     PM[2 + n].rearrange("p (h t) -> p h t", h=H))
                last.then_inc(s["level_read"], 1)

            def keep(l, product, level, bank):
                m = LEVELS[level]
                dve.wait_ge(s["level_read"], 11 * l + product - 1)
                dve.sem_inc(s["dve_passed"], 1)
                dve.wait_ge(s["level_mm"], 11 * l + product)
                dve.sem_inc(s["dve_passed"], 1)
                out = ktok.rearrange("p (c a e s) -> p c a e s", c=NB * H, e=2, s=m)[:, :, :, 1, :]
                mask = lmask[:, level].rearrange("p (o a e s) -> p o a e s", o=1, e=2, s=m)[:, :, :, 1, :]
                z = PM[bank].rearrange("p (c a s) -> p c a s", c=NB * H, s=m)
                nc.vector.copy_predicated(out, mask.to_broadcast(list(z.shape)), z).then_inc(s["level_read"], 1)

            def keep_sample(l, product, level, bank):
                dve.wait_ge(s["level_read"], 11 * l + product - 1)
                dve.sem_inc(s["dve_passed"], 1)
                dve.wait_ge(s["level_mm"], 11 * l + product)
                dve.sem_inc(s["dve_passed"], 1)
                dve.wait_ge(s["lmask_ready"], 1)
                last = nc.vector.copy_predicated(ATsv[0:NS], bc(lmask[0:NS, level, 0:NS], H),
                                                 PM[bank][0:NS, 0:H * NS].rearrange("p (h t) -> p h t", h=H))
                last.then_inc(s["level_read"], 1)

            def branches(l, u):
                n, half = 2 - (u - U_BR) // 4, (u - U_BR) % 4
                for k in range(2):
                    d = 2 * half + k
                    t = T_BR + 2 * (u - U_BR) + k
                    if k == 0:
                        dve.wait_ge(s["half_done"], 12 * l + (u - U_BR + 1))
                    else:
                        dve.wait_ge(s["unit_done"], l * UNITS + (u + 1) + HEAD)
                    dve.wait_ge(s["gate"], 3 * l + (3 - n))
                    tt(gates[:, n, d], gates[:, n, d], PZ[t % 4][:, 0:T], ALU.mult).then_inc(s["z_read_dve"], 1)
                    if n == 0 and d >= KT - 2:
                        dve.wait_ge(s["z_read_dve"], read_dve(l, t))
                        dve.wait_ge(s["acc"], l * KT + (d + 1))
                        tt(gates[:, 2, d], gates[:, 2, d], gates[:, 0, d], ALU.add).then_inc(s["merged_late"], 1)

            def merged_lo(l, ds_):
                for d in ds_:
                    dve.wait_ge(s["m_hi"], l * KT + (d + 1))
                    tt(h_lo[:, d], gates[:, 2, d], f(h_hi[:, d]), ALU.subtract).then_inc(s["m_lo"], 1)

            def mlp(l, i, last, first=False):
                for j in range(16):
                    if j < 8:
                        dve.wait_ge(s["unit_done"], l * UNITS + i * 16 + (U_FFN + j + 1) + HEAD)
                        if first and j == 0:
                            dve.wait_ge(s["rstd"], 2 * l + 2)
                        dve.wait_ge(s["hsq"], l * 8 * FI + i * 8 + max(j - 1, 0) + HEAD)
                        stt(relu[:, j % 2], PZ[(T_FFN + j) % 4][:, 0:T], 0.0, rstd[:], ALU.max,
                            ALU.mult).then_inc(s["z_read_dve"], 1)
                    for d in {0: (), 7: (6, 7)}.get(j, (j - 1,) if j < 8 else ()):
                        dve.wait_ge(s["f_hi"], l * 8 * FI + i * 8 + (d + 1))
                        tt(h_lo[:, d], hsq[:, d % 2], f(h_hi[:, d]), ALU.subtract).then_inc(s["f_lo"], 1)
                    if j >= 8:
                        add_to_x(l, j - 8, PZ[(T_FFN + j) % 4], l * UNITS + i * 16 + (U_FFN + j + 1))
                    if j + LEAD < 16 or not last:
                        split(l, U_FFN + j + LEAD, i)
                    if last and j == 15:
                        split(l + 1, 0)
                    if last and j >= 8:
                        input_lo(2 * l + 3, j - 8, lambda k: pr("norm_next", k))
                        add_square(2 * l + 3, j - 8)
                if last:
                    for u in range(1, LEAD):
                        split(l + 1, u)

            for name in ("w_lo", "z_read_dve", "ssum", "hsq", "f_lo", "oa_lo", "snew_read"):
                dve.sem_inc(s[name], HEAD)
            dve.wait_ge(s["params_landed"], 16)
            lbs = params[:, :, PAR["lb"][0]:PAR["lb"][0] + H]
            e = small[:, 0:2 * H].rearrange("p (l h) -> p l h", l=DEPTH)
            prep = Chain(dve, "prep_chain", 0)
            t = lambda k: small[:, 16 + 4 * k:20 + 4 * k]
            bm = lambda a: bc(a, DEPTH)
            lower = small[:, 64:64 + DEPTH * H].rearrange("p (l h) -> p l h", l=DEPTH)
            prep(tt(t(0), lbs[:, 0], lbs[:, 1], ALU.max))
            prep(tt(e, lbs, bm(t(0)), ALU.subtract))
            dve.sem_inc(s["prep_v"], 1)
            dve.wait_ge(s["prep_a"], 1)
            prep(tt(t(1), e[:, 0], e[:, 1], ALU.add))
            prep(nc.vector.reciprocal(t(2), t(1)))
            prep(tt(e, e, bm(t(2)), ALU.mult))
            prep(nc.vector.tensor_copy(lower[:, 0], e[:, 0]))
            for k in range(1, DEPTH):
                prep(tt(lower[:, k], lower[:, k - 1], e[:, k], ALU.add))
            prep(tt(lower, lower, bm(e[:, 0]), ALU.subtract))
            prep(ts_(lower, lower, 0.0, None, ALU.max))
            om, log_om, log_lb = (params[:, :, PAR[n][0]:PAR[n][0] + H] for n in ("om", "log_om", "log_lb"))
            prep(ts_(om, lower, -1.0, 1.0, ALU.mult, ALU.add))
            tiny = 2.0 ** -60
            logs = small[:, 32:32 + 3 * DEPTH * H].rearrange("p (n l h) -> p n l h", n=3, l=DEPTH)
            prep(ts_(logs[:, 0], om, tiny, None, ALU.max))
            prep(ts_(logs[:, 1], lower, LB_FLOOR, tiny, ALU.max, ALU.max))
            prep(ts_(lower, lower, LB_FLOOR, 1.0 / tiny, ALU.max, ALU.mult))
            ts_(logs[:, 2], lower, 1.0, None, ALU.min).then_inc(s["prep_v"], 1)
            dve.wait_ge(s["prep_a"], 2)
            nc.vector.tensor_copy(log_om, logs[:, 0])
            prep(tt(log_lb, logs[:, 1], logs[:, 2], ALU.add))
            for j in range(KT):
                if j % 4 == 0:
                    dve.wait_ge(s[f"x_landed{j}"], 16)
                input_lo(1, j, first_norm)
                if j == 3:
                    split(0, 0)
            split(0, 1)
            for j in range(KT):
                add_square(1, j)
            split(0, 2)
            dve.wait_ge(s["consts_landed"], 16)
            with dve.Fori(0, DEPTH) as l:
                chain.layer(l * DVE_CHAIN)
                dve.wait_ge(s["a_lo"], 16 * l + KT)
                chain(nc.vector.tensor_copy(par[:], params[:, bass.ds(l, 1), :].rearrange("p o n -> p (o n)")))
                for u in range(U_FFN):
                    if u < U_GATE:
                        read_tile(l, u)
                    if U_BR <= u < U_O:
                        branches(l, u)
                    if u >= U_O:
                        add_to_x(l, u - U_O, PZ[(T_O + u - U_O) % 4], l * UNITS + (u + 1))
                    late_split = u in (10, 18, 19, 28) or u >= U_O - 1
                    if not late_split:
                        split(l, u + LEAD)
                    if U_BR + 8 <= u < U_O:
                        merged_lo(l, (2 * (u - U_BR - 8), 2 * (u - U_BR - 8) + 1))
                    attention(l, u)
                    pooling(l, u)
                    hgrn(l, u)
                    if u >= U_O:
                        input_lo(2 * l + 2, u - U_O, lambda k: pr("norm_ffn", k))
                        add_square(2 * l + 2, u - U_O)
                    if late_split:
                        split(l, u + LEAD)
                with dve.Fori(0, FI - 1) as i:
                    mlp(l, i, False, True)
                mlp(l, FI - 1, True)
                assert chain.k == DVE_CHAIN, chain.k

        @block.gpsimd
        def _(pool):
            chain = Chain(pool, "pool_chain", 0)
            pool.wait_ge(s["consts_landed"], 16)
            pool.dma_start(A[:, 4096:4096 + lmask.shape[1] * P], io["lmask"]).then_inc(s["lmask_landed"], 16)
            pool.wait_ge(s["lmask_landed"], 16)
            nc.gpsimd.tensor_copy(lmask[:].rearrange("p l t -> p (l t)"),
                                  A[:, 4096:4096 + lmask.shape[1] * P]).then_inc(s["lmask_ready"], 1)
            tt = nc.gpsimd.tensor_tensor
            pool.sem_inc(s["s0_free"], HEAD)
            pool.dma_start(io["kc_out"], io["kc_kept"]).then_inc(s["cache_out"], 16)
            pool.dma_start(io["vc_out"], io["vc_kept"]).then_inc(s["cache_out"], 16)
            pool.wait_ge(s["consts_landed"], 16)
            with pool.Fori(0, DEPTH) as l:
                chain.layer(l * POOL_CHAIN)
                pool.wait_ge(s["qk_norm"], 2 * l + 2)
                pool.wait_ge(s["cos_sin_landed"], 16 * (l + 1))
                q5 = qk.rearrange("p (j t) -> p j t", t=T)
                tt(qk_rs.rearrange("p (j t) -> p j t", t=T), q5, bc(cos, 5), ALU.mult).then_inc(s["qk_cos"], 1)
                nc.gpsimd.memset(uext[:, :, 0:PAD], 0.0).then_inc(s["u_front"], 1)
                chain(nc.gpsimd.memset(q_samp, 0.0))
                pool.wait_ge(s["qk_rope"], l + 1)
                pool.wait_ge(s["u_front"], l + 1)
                pool.sem_inc(s["pool_passed"], 1)
                for kv in range(KV):
                    if kv:
                        pool.wait_ge(s["q_samp"], 2 * l + kv)
                        pool.sem_inc(s["pool_passed"], 1)
                    rows = slice(kv * HD, (kv + 1) * HD)
                    o = q_samp.rearrange("p (b k j t) -> p b k j t", b=B, k=KV, j=GRP)[rows, :, kv]
                    i_ = q5[rows, 0:4, NP:T].rearrange("p j (b t) -> p b j t", t=TS)
                    nc.gpsimd.tensor_copy(o, i_).then_inc(s["q_samp"], 1)
                pool.wait_ge(s["q_samp"], 2 * l + 2)
                pool.dma_start(io["k_out"][l], qk[:, 4 * T:]).then_inc(s["kv_out"], 16)
                pool.dma_start(io["v_out"][l], vz).then_inc(s["kv_out"], 16)
                pool.wait_ge(s["z_read_dve"], read_dve(l, U_U + 3))
                pool.wait_ge(s["ustate_landed"], 16 * (l + 1))
                pool.wait_ge(s["u_front"], l + 1)
                pool.dma_start(io["u_out"][l], S0[:, 0:G4 * UX]).then_inc(s["u_out"], 16)
                chain(tt(wa[:, :, 1:], uext[:, :, 1:], uext[:, :, :-1], ALU.add))
                chain(tt(wb[:, :, 3:], wa[:, 1:4, 3:], wa[:, 1:4, 1:-2], ALU.add))
                chain(tt(wa[:, 2:4, 7:], wb[:, 1:3, 7:], wb[:, 1:3, 3:-4], ALU.add))
                chain(tt(wb[:, 2, 15:], wa[:, 3, 15:], wa[:, 3, 7:-8], ALU.add))
                for g in range(G4):
                    last = tt(first[:, g], wsum[g][:, PAD:2 * PAD],
                              c("invcnt").rearrange("p (g n) -> p g n", g=G4)[:, g], ALU.mult)
                last.then_inc(s["wsum"], 1)
                pool.wait_ge(s["wsum"], l + 1)
                tt(pool_d[:, :, 0:PAD], first, uext[:, :, PAD:2 * PAD], ALU.subtract).then_inc(s["pool_first"], 2)
                pool.wait_ge(s["rec"], l + 1)
                for g in range(7):
                    if g < 6:
                        hs, o = (GRP, g * 4) if g < 2 else (2, 8 + 2 * (g - 2))
                        a = prob[:, g].rearrange("p (a n) -> p a n", a=hs)
                    else:
                        hs, o, a = 2, 16, p_samp
                    tt(a, a, bl(rec[:, o:o + hs], a.shape[2]), ALU.mult).then_inc(s["prob_n"], 1)
                pool.wait_ge(s["sig"], 3 * l + 1)
                tt(ZQ, ZQ, D0, ALU.mult).then_inc(s["hz_q"], 1)
                pool.wait_ge(s["sig"], 3 * l + 3)
                tt(ZG, ZG, D1, ALU.mult).then_inc(s["silu_g"], 1)

                def scale_gates(n):
                    pool.wait_ge(s["z_read_act"], read_act(l, U_GATE + (3 - n) * KT - 1))
                    tt(gates[:, n], gates[:, n], bc(rstd[:], KT), ALU.mult).then_inc(s["gate_z"], 1)

                pool.wait_ge(s["sfin"], l + 1)
                pool.sem_inc(s["pool_passed"], 1)
                nc.gpsimd.memset(AT[:], 0.0).then_inc(s["at_zero"], 1)
                nc.gpsimd.memset(ATs, 0.0).then_inc(s["at_zero"], 1)
                pool.wait_ge(s["sfin_read"], l + 1)
                pool.dma_start(io["sp_out"][l].rearrange("p h n -> p (h n)"), ZI[:, 0:512]).then_inc(s["sp_out"], 16)
                scale_gates(2)
                pool.wait_ge(s["s0_q"], 4 * (l + 1))
                tt(S0.rearrange("p (b n) -> p b n", n=P), S0.rearrange("p (b n) -> p b n", n=P), bl(es, P),
                   ALU.mult).then_inc(s["s0_decay"], 1)
                scale_gates(1)
                scale_gates(0)
                pool.wait_ge(s["o_ps"], 3 * l + 3)
                for h in range(H):
                    im = (KK, D1, X1, ZF)[h][0:NS, 0:B * P].rearrange("p (b n) -> p b n", b=B)
                    tt(im, bc(itok[0:NS, 2, h], B), bl(c("bmask", slice(0, NS)), P), ALU.mult).then_inc(s["imask"], 1)
                for d in range(KT):
                    pool.wait_ge(s["z_read_dve"], read_dve(l, T_BR + KT + d))
                    tt(gates[:, 2, d], gates[:, 2, d], gates[:, 1, d], ALU.add).then_inc(s["acc"], 1)
                pool.wait_ge(s["acc"], (l + 1) * KT)
                for d in range(KT - 2):
                    pool.wait_ge(s["z_read_dve"], read_dve(l, T_BR + 2 * KT + d))
                    tt(gates[:, 2, d], gates[:, 2, d], gates[:, 0, d], ALU.add).then_inc(s["merged"], 1)
                pool.wait_ge(s["snew_read"], 4 * l + 4 + HEAD)
                pool.dma_start(io["ss_out"][l].rearrange("p b n -> p (b n)"), S0).then_inc(s["ss_out"], 16)
                pool.wait_ge(s["ss_out"], 16 * (l + 1))
                pool.sem_inc(s["s0_free"], 1)
                assert chain.k == POOL_CHAIN, chain.k
            for name, n in (("cache_out", 32), ("kv_out", 32 * DEPTH), ("u_out", 16 * DEPTH),
                            ("sp_out", 16 * DEPTH), ("ss_out", 16 * DEPTH)):
                pool.wait_ge(s[name], n)


DVE_CHAIN = 13
POOL_CHAIN = 5


def _weights(w_in, w_branch, w_o, w_up, w_down):
    stream = np.zeros((DEPTH * UNITS + RING, P, UW), w_in.dtype)
    out = stream[:DEPTH * UNITS].reshape(DEPTH, UNITS, P, UW)

    def tiles(w):
        k, n = w.shape
        return w.reshape(k // P, P, n // P, P).transpose(2, 1, 0, 3)

    for l in range(DEPTH):
        w = w_in[l]
        q = w[:, 0:512].reshape(D_MODEL, KV, GRP, HD).transpose(0, 2, 1, 3).reshape(D_MODEL, 512)
        kv, hq, hf, hi, hg, u = (w[:, a:b] for a, b in (
            (512, 768), (768, 1280), (1280, 1792), (1792, 2304), (2304, 2816), (2816, 3328)))
        z = [w[:, 3328 + n * D_MODEL:3328 + (n + 1) * D_MODEL] for n in (2, 1, 0)]
        a = np.concatenate([q, kv, u, hf, hq, hi, hg] + z, 1)
        out[l, 0:U_BR] = tiles(a).reshape(U_BR, P, UW)
        for i, n in enumerate((2, 1, 0)):
            wb = w_branch[l, n]
            if n == 1:
                wb = wb.reshape(KV, GRP, HD, D_MODEL).transpose(1, 0, 2, 3).reshape(512, D_MODEL)
            out[l, U_BR + 4 * i:U_BR + 4 * i + 4] = (
                wb.reshape(4, P, 4, 256).transpose(2, 1, 0, 3).reshape(4, P, UW))
        out[l, U_O:U_FFN] = tiles(w_o[l]).reshape(8, P, UW)
        up = tiles(w_up[l]).reshape(FI, 8, P, UW)
        down = w_down[l].reshape(FI, KT, P, KT, P).transpose(0, 3, 2, 1, 4).reshape(FI, 8, P, UW)
        out[l, U_FFN:] = np.concatenate([up, down], 1).reshape(FI * 16, P, UW)
    return stream


def _params(d):
    def col(a):
        return np.asarray(a).reshape(-1, P).T

    rows = []
    for l in range(DEPTH):
        sink = np.asarray(d["attn_sinks"][l])
        rows.append(np.concatenate([
            col(d["norm_mix"][(l + 1) % DEPTH]), col(d["norm_ffn"][l]),
            np.tile(d["q_norm"][l], 2)[:, None], np.tile(d["k_norm"][l], 2)[:, None],
            np.tile(sink[None], (P, 1)), np.tile(np.repeat(sink, TS), 4)[:, None],
            np.asarray(d["hgrn_onorm"][l])[:, None], col(d["pool_scale"][l]), col(d["hgrn_lb"][l])], 1))
    return np.ascontiguousarray(np.stack(rows, 1))


def kernel(**inputs):
    import concourse.bacc as _bacc
    from concourse.bass_utils import run_bass_kernel_spmd as _run

    d = {k: np.asarray(v) for k, v in inputs.items()}
    con, cos_sin = _constants()
    xs = d["x_sample"].reshape(NS, D_MODEL)
    xt = np.concatenate([d["x_prompt"].reshape(NP, D_MODEL), xs], 0)
    kc, vcache = (d[k].reshape(DEPTH, B, P, P) for k in ("cache_swa_k", "cache_swa_v"))
    state = np.zeros((DEPTH, P, G4, B, SEG), d["state_pool"].dtype)
    state[..., 1:PAD] = d["state_pool"].reshape(DEPTH, B, PAD - 1, G4, P).transpose(0, 4, 3, 1, 2)
    arrays = {
        "x_in": xt.reshape(T, KT, P).transpose(2, 1, 0),
        "w": _weights(d["w_in"], d["w_branch"], d["w_o"], d["w_up"], d["w_down"]),
        "params": _params(d),
        "consts": con,
        "cos_sin": cos_sin,
        "lmask": _level_masks(),
        "kcT": kc.transpose(0, 3, 1, 2),
        "vc": vcache.transpose(0, 2, 1, 3),
        "pool_w": d["pool_w"].transpose(0, 2, 1, 3),
        "pool_state": state.reshape(DEPTH, P, G4, B * SEG),
        "s0": d["state_hgrn"].transpose(0, 3, 1, 2, 4).reshape(DEPTH, P, B * H * P),
        "kc_kept": kc[:, :, TS:].reshape(DEPTH * B, (P - TS) * P),
        "vc_kept": vcache[:, :, TS:].reshape(DEPTH * B, (P - TS) * P),
    }
    nc = _bacc.Bacc("TRN2", target_bir_lowering=False, num_devices=1)
    io, sent = {}, {}
    for name, a in arrays.items():
        a = np.ascontiguousarray(a)
        sent[f"in_{name}"] = a
        io[name] = nc.dram_tensor(f"in_{name}", a.shape, mybir.dt.from_np(a.dtype), kind="ExternalInput").ap()
    for name, shape in OUT_SHAPES.items():
        io[name] = nc.dram_tensor(f"out_{name}", shape, F32, kind="ExternalOutput").ap()
    build(nc, io)
    r = _run(nc, [sent], core_ids=[0]).results[0]
    got = {name: r[f"out_{name}"] for name in OUT_SHAPES}

    y = got["y"].transpose(2, 1, 0).reshape(T, D_MODEL)
    ko, vo = got["k_out"], got["v_out"]
    heads = (KV, HD)

    def cache(kept, new):
        k = kept.reshape(DEPTH, B, P - TS, P)
        n = new[:, :, NP:].reshape(DEPTH, P, B, TS).transpose(0, 2, 3, 1)
        return np.concatenate([k, n], 2).reshape(DEPTH, B, P, *heads)

    def prompt_cache(a):
        return np.ascontiguousarray(a[:, :, NP - P:NP].transpose(0, 2, 1)).reshape(DEPTH, 1, P, *heads)

    u = got["u_out"].reshape(DEPTH, P, G4, UX)
    pool_p = u[..., PAD + NP - 15:PAD + NP].transpose(0, 3, 2, 1).reshape(DEPTH, 1, 15, G4 * P)
    pool_s = u[..., PAD + NP:].reshape(DEPTH, P, G4, B, SEG)[..., SEG - 15:]
    pool_s = pool_s.transpose(0, 3, 4, 2, 1).reshape(DEPTH, B, 15, G4 * P)
    sp_ = got["sp_out"].transpose(0, 2, 1, 3).reshape(DEPTH, 1, H, P, P)
    ss_ = got["ss_out"].reshape(DEPTH, P, B, H, P).transpose(0, 2, 3, 1, 4)
    c_ = np.ascontiguousarray
    return (c_(y[:NP]).reshape(1, NP, D_MODEL), c_(y[NP:]).reshape(B, TS, D_MODEL),
            c_(sp_), prompt_cache(ko), prompt_cache(vo), c_(pool_p),
            c_(ss_), cache(got["kc_out"], ko), cache(got["vc_out"], vo), c_(pool_s))
```
